# Optimizing a Trainium2 kernel written in Bass

```python
import jax, jax.numpy as jnp
from jax import lax
import numpy as np

D_MODEL = 1024
BATCH = 1
SEQ = 512
DEPTH = 1

CHUNK = 64
Q_BLOCK = 128
MLA_HEADS = 8
QK_NOPE_DIM = 64
QK_ROPE_DIM = 32
QK_HEAD_DIM = QK_NOPE_DIM + QK_ROPE_DIM
V_HEAD_DIM = 64
Q_LORA_RANK = 384
KV_LORA_RANK = 128
ROPE_THETA = 10000.0
ATTN_WIDTH = MLA_HEADS * V_HEAD_DIM
CONV_WIDTH = D_MODEL - ATTN_WIDTH
CONV_KERNEL = 31
IN_WIDTH = Q_LORA_RANK + KV_LORA_RANK + QK_ROPE_DIM + 2 * CONV_WIDTH
N_EXPERTS = 32
TOP_K = 4
D_FF = D_MODEL
SWIGLU_ALPHA = 1.702
SWIGLU_LIMIT = 7.0
MOE_BLOCK = 256
EPS = 1e-6

kernel_name = "hybrid_mla_conformer_moe_block"

def rms_norm(x, g):
    xf = x.astype(jnp.float32)
    y = xf * lax.rsqrt(jnp.mean(xf * xf, axis=-1, keepdims=True) + EPS)
    return (y * g.astype(jnp.float32)).astype(x.dtype)

def layer_norm(x, g, b):
    xf = x.astype(jnp.float32)
    mu = jnp.mean(xf, axis=-1, keepdims=True)
    xc = xf - mu
    y = xc * lax.rsqrt(jnp.mean(xc * xc, axis=-1, keepdims=True) + EPS)
    return (y * g.astype(jnp.float32) + b.astype(jnp.float32)).astype(x.dtype)

def rope_tables(positions):
    inv_freq = 1.0 / (ROPE_THETA ** (jnp.arange(0, QK_ROPE_DIM, 2, dtype=jnp.float32) / QK_ROPE_DIM))
    ang = positions.astype(jnp.float32)[..., None] * inv_freq
    return jnp.cos(ang)[:, :, None, :], jnp.sin(ang)[:, :, None, :]

def rope_tail(t, cos, sin):
    nope, pe = t[..., :QK_NOPE_DIM], t[..., QK_NOPE_DIM:].astype(jnp.float32)
    half = QK_ROPE_DIM // 2
    x1, x2 = pe[..., :half], pe[..., half:]
    rot = jnp.concatenate([x1 * cos - x2 * sin, x2 * cos + x1 * sin], axis=-1)
    return jnp.concatenate([nope, rot.astype(t.dtype)], axis=-1)

def attend_block(qb, kb, vb, q0):
    scale = QK_HEAD_DIM ** -0.5
    s = jnp.einsum('bqhd,bkhd->bhqk', qb, kb, preferred_element_type=jnp.float32) * scale
    q_chunk = (q0 + jnp.arange(qb.shape[1])) // CHUNK
    k_chunk = jnp.arange(kb.shape[1]) // CHUNK
    s = jnp.where(k_chunk[None, :] <= q_chunk[:, None], s, -jnp.inf)
    p = jax.nn.softmax(s, axis=-1).astype(vb.dtype)
    return jnp.einsum('bhqk,bkhd->bqhd', p, vb)

def mla(c_q, c_kv, k_pe, cos, sin, q_latent_g, w_uq, kv_latent_g, w_ukv, q_head_g, k_head_g):
    B, S, _ = c_q.shape
    q = (rms_norm(c_q, q_latent_g) @ w_uq).reshape(B, S, MLA_HEADS, QK_HEAD_DIM)
    kv = (rms_norm(c_kv, kv_latent_g) @ w_ukv).reshape(B, S, MLA_HEADS, QK_NOPE_DIM + V_HEAD_DIM)
    k_nope, v = kv[..., :QK_NOPE_DIM], kv[..., QK_NOPE_DIM:]
    k = jnp.concatenate(
        [k_nope, jnp.broadcast_to(k_pe[:, :, None, :], (B, S, MLA_HEADS, QK_ROPE_DIM))], axis=-1)
    q = rope_tail(rms_norm(q, q_head_g), cos, sin)
    k = rope_tail(rms_norm(k, k_head_g), cos, sin)
    outs = []
    for i in range(S // Q_BLOCK):
        q0, end = i * Q_BLOCK, (i + 1) * Q_BLOCK
        outs.append(attend_block(q[:, q0:end], k[:, :end], v[:, :end], q0))
    return jnp.concatenate(outs, axis=1).reshape(B, S, ATTN_WIDTH)

def conformer_conv(u, dw_w, dw_b, ln_g, ln_b):
    a, g = u[..., :CONV_WIDTH], u[..., CONV_WIDTH:]
    y = a * jax.nn.sigmoid(g)
    y = lax.conv_general_dilated(
        y, dw_w[:, None, :].astype(y.dtype), window_strides=(1,),
        padding=[(CONV_KERNEL - 1, 0)], dimension_numbers=('NWC', 'WIO', 'NWC'),
        feature_group_count=CONV_WIDTH) + dw_b
    return jax.nn.silu(layer_norm(y, ln_g, ln_b))

def moe(h, router_w, router_b, w_gate_up, b_gate_up, w_down, b_down):
    B, S, D = h.shape
    T = B * S
    hf = h.reshape(T, D)
    logits = (hf @ router_w).astype(jnp.float32) + router_b.astype(jnp.float32)
    top_val, top_idx = lax.top_k(logits, TOP_K)
    gates = jax.nn.softmax(top_val, axis=-1)
    n_assign = T * TOP_K
    flat_e = top_idx.reshape(-1).astype(jnp.int32)
    flat_tok = jnp.arange(n_assign, dtype=jnp.int32) // TOP_K
    order = jnp.argsort(flat_e)
    se, stok, sw = flat_e[order], flat_tok[order], gates.reshape(-1)[order]
    counts = jnp.bincount(flat_e, length=N_EXPERTS)
    starts = jnp.cumsum(counts) - counts
    pcounts = (counts + MOE_BLOCK - 1) // MOE_BLOCK * MOE_BLOCK
    pends = jnp.cumsum(pcounts)
    pstarts = pends - pcounts
    dest = pstarts[se] + jnp.arange(n_assign, dtype=jnp.int32) - starts[se]
    P = n_assign + N_EXPERTS * MOE_BLOCK
    n_blocks = P // MOE_BLOCK
    slot_tok = jnp.full((P,), T, jnp.int32).at[dest].set(stok)
    slot_w = jnp.zeros((P,), jnp.float32).at[dest].set(sw)
    block_e = jnp.minimum(
        jnp.searchsorted(pends, jnp.arange(n_blocks) * MOE_BLOCK, side='right'), N_EXPERTS - 1)
    x_pad = jnp.concatenate([hf, jnp.zeros((1, D), hf.dtype)], axis=0)
    xs = x_pad[slot_tok].reshape(n_blocks, MOE_BLOCK, D)

    def expert_block(args):
        xb, e = args
        gu = xb @ w_gate_up[e] + b_gate_up[e]
        gate = jnp.minimum(gu[:, :D_FF], SWIGLU_LIMIT)
        up = jnp.clip(gu[:, D_FF:], -SWIGLU_LIMIT, SWIGLU_LIMIT)
        glu = gate * jax.nn.sigmoid(gate * SWIGLU_ALPHA)
        return ((up + 1.0) * glu) @ w_down[e] + b_down[e]

    ys = lax.map(expert_block, (xs, block_e)).reshape(P, D)
    out = jnp.zeros((T + 1, D), jnp.float32).at[slot_tok].add(ys.astype(jnp.float32) * slot_w[:, None])
    return out[:T].astype(h.dtype).reshape(B, S, D)

def setup_inputs(seed: int = 0) -> dict:
    key = jax.random.key(seed)
    ks = jax.random.split(key, 26)
    L = DEPTH
    f32 = jnp.float32

    def w(k, shape, fan_in):
        return jax.random.normal(k, shape, f32) * (fan_in ** -0.5)

    def gain(k, shape):
        return 1.0 + 0.02 * jax.random.normal(k, shape, f32)

    def bias(k, shape):
        return 0.01 * jax.random.normal(k, shape, f32)

    start = jax.random.randint(ks[1], (BATCH, 1), 0, 65536, dtype=jnp.int32)
    return {
        "x": jax.random.normal(ks[0], (BATCH, SEQ, D_MODEL), f32),
        "positions": start + jnp.arange(SEQ, dtype=jnp.int32)[None, :],
        "norm_mix_g": gain(ks[2], (L, D_MODEL)),
        "w_in": w(ks[3], (L, D_MODEL, IN_WIDTH), D_MODEL),
        "q_latent_g": gain(ks[4], (L, Q_LORA_RANK)),
        "w_uq": w(ks[5], (L, Q_LORA_RANK, MLA_HEADS * QK_HEAD_DIM), Q_LORA_RANK),
        "kv_latent_g": gain(ks[6], (L, KV_LORA_RANK)),
        "w_ukv": w(ks[7], (L, KV_LORA_RANK, MLA_HEADS * (QK_NOPE_DIM + V_HEAD_DIM)), KV_LORA_RANK),
        "q_head_g": gain(ks[8], (L, QK_HEAD_DIM)),
        "k_head_g": gain(ks[9], (L, QK_HEAD_DIM)),
        "conv_dw_w": w(ks[10], (L, CONV_KERNEL, CONV_WIDTH), CONV_KERNEL),
        "conv_dw_b": bias(ks[11], (L, CONV_WIDTH)),
        "conv_ln_g": gain(ks[12], (L, CONV_WIDTH)),
        "conv_ln_b": bias(ks[13], (L, CONV_WIDTH)),
        "attn_out_g": gain(ks[14], (L, ATTN_WIDTH)),
        "conv_out_g": gain(ks[15], (L, CONV_WIDTH)),
        "w_out": w(ks[16], (L, D_MODEL, D_MODEL), D_MODEL),
        "norm_ffn_g": gain(ks[17], (L, D_MODEL)),
        "router_w": w(ks[18], (L, D_MODEL, N_EXPERTS), D_MODEL),
        "router_b": bias(ks[19], (L, N_EXPERTS)),
        "w_gate_up": w(ks[20], (L, N_EXPERTS, D_MODEL, 2 * D_FF), D_MODEL),
        "b_gate_up": bias(ks[21], (L, N_EXPERTS, 2 * D_FF)),
        "w_down": w(ks[22], (L, N_EXPERTS, D_FF, D_MODEL), D_FF),
        "b_down": bias(ks[23], (L, N_EXPERTS, D_MODEL)),
    }

def reference(x, positions, norm_mix_g, w_in, q_latent_g, w_uq, kv_latent_g, w_ukv, q_head_g,
              k_head_g, conv_dw_w, conv_dw_b, conv_ln_g, conv_ln_b, attn_out_g, conv_out_g, w_out,
              norm_ffn_g, router_w, router_b, w_gate_up, b_gate_up, w_down, b_down):
    cos, sin = rope_tables(positions)
    o1 = Q_LORA_RANK
    o2 = o1 + KV_LORA_RANK
    o3 = o2 + QK_ROPE_DIM
    for l in range(DEPTH):
        h = rms_norm(x, norm_mix_g[l])
        p = h @ w_in[l]
        attn = mla(p[..., :o1], p[..., o1:o2], p[..., o2:o3], cos, sin,
                   q_latent_g[l], w_uq[l], kv_latent_g[l], w_ukv[l], q_head_g[l], k_head_g[l])
        conv = conformer_conv(p[..., o3:], conv_dw_w[l], conv_dw_b[l], conv_ln_g[l], conv_ln_b[l])
        mixed = jnp.concatenate([rms_norm(attn, attn_out_g[l]), rms_norm(conv, conv_out_g[l])], axis=-1)
        x = x + mixed @ w_out[l]
        h = rms_norm(x, norm_ffn_g[l])
        x = x + moe(h, router_w[l], router_b[l], w_gate_up[l], b_gate_up[l], w_down[l], b_down[l])
    return x


_drawn_inputs = setup_inputs


def setup_inputs(seed=0):
    import zlib

    import numpy as np

    out = dict(_drawn_inputs(seed))
    spreads = {}
    factors = {'conv_ln_b': 3.908, 'b_gate_up': 8.0, 'b_down': 8.0}
    for name, (base, spread) in spreads.items():
        noise = np.random.default_rng([zlib.crc32(name.encode()), seed]).standard_normal(out[name].shape)
        drawn = base * np.exp(spread * noise) if base else spread * noise
        out[name] = __import__('jax').numpy.asarray(drawn.astype(out[name].dtype))
    for name, factor in factors.items():
        out[name] = (out[name] * factor).astype(out[name].dtype)
    return out
```

```python
from contextlib import ExitStack

import numpy as np
import concourse.bass as bass
from concourse import mybir

F32 = mybir.dt.float32
I32 = mybir.dt.int32
U32 = mybir.dt.uint32
ALU = mybir.AluOpType
ACT = mybir.ActivationFunctionType
AX = mybir.AxisListType

P = 128
T = 512
TT = T // P
D = 1024
DK = D // P
Q_RANK, KV_RANK = 384, 128
QJ = Q_RANK // P
H, NOPE, ROPE, VD = 8, 64, 32, 64
HD = NOPE + ROPE
CONV = 512
CC = CONV // P
TAPS = 31
PAD = TAPS - 1
IN_W = Q_RANK + KV_RANK + ROPE + 2 * CONV
COL_ROPE = Q_RANK + KV_RANK
COL_A = COL_ROPE + ROPE
COL_G = COL_A + CONV
CHUNK = 64
E, TOPK, FF = 32, 4, 1024
EPS = 1e-6
SCALE = HD ** -0.5
ALPHA, LIMIT = 1.702, 7.0
MAX_TILES = E + (T * TOPK - 1) // P
TAB = 48
TAB_E, TAB_J, TAB_N, TAB_T = 0, TAB, 2 * TAB, 3 * TAB
NONE = 4096.0
SLOT_BYTES = 8192
GU_CHUNKS, DN_CHUNKS = 8, 4
CHUNKS = GU_CHUNKS + DN_CHUNKS

V_MIX, V_QL, V_KL, V_DWB, V_LNG, V_LNB, V_AG, V_CG, V_FG, V_W = 0, 8, 11, 12, 16, 20, 24, 28, 32, 40
V_POS = V_W + TAPS * CC
V_ALL = V_POS + TT

TWO_PI = 2.0 * np.pi
PI2_A = 6.28125
PI2_B = float(np.round((TWO_PI - PI2_A) * 2.0 ** 19) / 2.0 ** 19)
PI2_C = TWO_PI - PI2_A - PI2_B
ROUND = 1.5 * 2.0 ** 23
PI_IN = float(np.float32(3.1415925))


def block_kernel(nc, A):
    with ExitStack() as ctx:
        base = (nc.sbuf_base + 63) // 64 * 64
        fence = ctx.enter_context(nc.sbuf_tensor("arena", [P, 53000], F32))
        del fence

        def at(name, offset, shape, dt=F32):
            return nc.alloc_sbuf_tensor_at(name, shape, dt, offset=base + offset)

        def sem(name):
            return ctx.enter_context(nc.semaphore(name))

        ring = [at(f"ring{c}", c * SLOT_BYTES, [P, 2, 2, 512] if c < GU_CHUNKS else [P, 2, 1024])
                for c in range(CHUNKS)]
        w_in = at("w_in", 0, [P, DK, IN_W])
        w_uq = at("w_uq", 50176, [P, QJ, H * HD])
        w_ukv = at("w_ukv", 59392, [P, 1024])
        w_out = at("w_out", 8 * SLOT_BYTES, [P, DK, D])
        qT = at("qT", 0, [HD, H, T])
        kT = at("kT", 16384, [HD, H, T])
        lnsq = at("lnsq", 32768, [P, CC, T])
        rowsq = at("rowsq", 40960, [P, 2, H * HD])
        o = CHUNKS * SLOT_BYTES
        x = at("x", o, [P, TT, D]); o += 16384
        hT = at("hT", o, [P, DK, T])
        mixT = at("mixT", o, [P, DK, T]); o += 16384
        arena_moe = o
        ypad = at("ypad", o, [P, CC, PAD + T]); o += 8704
        cacc = at("cacc", o, [P, CC, T]); o += 8192
        xn = at("xn", o, [P, TT, D])
        latT = at("latT", o, [P, 4, T])
        attn_row = at("attn_row", o, [P, 2, T])
        latsq = at("latsq", o + 8192, [P, 4, T])
        h2T = at("h2T", o + 8192, [P, 2, DK, P]); o += 16384
        vrow = at("vrow", o, [P, TT, H * VD])
        hn = at("hn", o, [P, TT, D]); o += 8192
        sgl = at("sgl", o, [P, 2, T])
        rows = [at(f"rows{n}", o + 3072 * n, [P, H, HD]) for n in range(4)]
        probs = at("probs", o, [P, 2, T])
        probsT = at("probsT", o + 4096, [P, 2, 4, P])
        bgu_rows = at("bgu_rows", o + 4096, [P, 4, P])
        bdn_rows = at("bdn_rows", o + 6144, [P, 2, P])
        vec_rows = at("vec_rows", o + 7168, [V_W, P])
        dw_rows = at("dw_rows", o + 7680, [TAPS * CC, P])
        pos_i = at("pos_i", o + 8192, [TT, P], I32)
        pos_f = at("pos_f", o + 8704, [TT, P])
        o += 12288
        m = arena_moe
        onehot = at("onehot", m, [P, TT, P]); m += 2048
        xg = at("xg", m, [P, D]); m += 4096
        xT = at("xT", m, [P, DK, P]); m += 4096
        g_in = at("g_in", m, [P, 4, P]); m += 2048
        u_in = at("u_in", m, [P, 4, P]); m += 2048
        g_sig = at("g_sig", m, [P, 4, P]); m += 2048
        act_T = at("act_T", m, [P, 8, P]); m += 4096
        yT = at("yT", m, [P, DK, P]); m += 4096
        yrow = at("yrow", m, [P, D]); m += 4096
        assert m <= arena_moe + 8704 + 8192 + 16384

        def small(name, shape, dt=F32):
            nonlocal o
            n = int(np.prod(shape[1:])) * 4
            t = at(name, o, shape, dt)
            o += (n + 31) // 32 * 32
            return t

        ident = small("ident", [P, P])
        tri = small("tri", [P, P])
        ones = small("ones", [P, P])
        inv_c = small("inv_c", [P, P])
        iota_s = small("iota_s", [P, T])
        inv_freq = small("inv_freq", [P, ROPE // 2])
        tokv = small("tokv", [P, TT, 3])
        slot_row = small("slot_row", [P, 1])
        eidx = small("eidx", [E, 1])
        eps = small("eps", [P, 1])
        vcol = small("vcol", [P, V_ALL])
        biasT = small("biasT", [P, E, 24])
        bias_t = small("bias_t", [P, 24])
        qk_gain = small("qk_gain", [P, 2, HD])
        router = small("router", [P, DK, E])
        router_bias = small("router_bias", [P, E])
        ssx = small("ssx", [P, TT]); stdx = small("stdx", [P, TT]); rsx = small("rsx", [P, TT])
        ang = small("ang", [P, TT, 16]); turns = small("turns", [P, 2, TT, 16])
        red = small("red", [P, 2, TT, 16])
        cosd = small("cosd", [P, TT, 2, 16]); sin_ = small("sin_", [P, TT, 16]); nsin = small("nsin", [P, TT, 16])
        krope = small("krope", [P, TT, ROPE])
        lat_std = small("lat_std", [P, 8]); lat_rs = small("lat_rs", [P, 8])
        ln_std = small("ln_std", [P, T])
        css = small("css", [P, TT]); c_rs = small("c_rs", [P, TT])
        hss = small("hss", [P, 8, H]); hstd = small("hstd", [P, 8, H]); hrs = small("hrs", [P, 8, H])
        rtmp = small("rtmp", [P, 2, H, ROPE])
        mx = small("mx", [P, 32]); nmx = small("nmx", [P, 32]); den = small("den", [P, TT, H]); rden = small("rden", [P, TT, H])
        ass_ = small("ass", [P, TT]); astd = small("astd", [P, TT]); a_rs = small("a_rs", [P, TT])
        ss1 = small("ss1", [P, TT]); std1 = small("std1", [P, TT]); rs1 = small("rs1", [P, TT])
        logits = small("logits", [P, TT, E])
        top_v = small("top_v", [P, TT, 8]); top_i = small("top_i", [P, TT, 8], U32); top_f = small("top_f", [P, TT, 4])
        hot = at("hot", arena_moe, [P, 16, E])
        hotg = at("hotg", arena_moe + 2048, [P, 16, E])
        tg = small("tg", [P, TT, 4]); tgs = small("tgs", [P, TT]); tgr = small("tgr", [P, TT])
        mask = small("mask", [P, TT, E]); gate = small("gate", [P, TT, E]); posm = small("posm", [P, TT, E])
        cnt = small("cnt", [E, 4]); member = small("member", [E, TAB]); memj = small("memj", [E, TAB]); memn = small("memn", [E, TAB])
        tab = small("tab", [1, 4 * TAB], I32)
        slot_f = small("slot_f", [P, 2])
        gate_next = small("gate_next", [P, 1]); idx_next = small("idx_next", [P, 1], I32)
        gate_cur = small("gate_cur", [P, 1]); idx_cur = small("idx_cur", [P, 1], I32)
        gate_hold = small("gate_hold", [P, 1]); idx_hold = small("idx_hold", [P, 1], I32)
        assert o <= 53000 * 4, o

        ps = ctx.enter_context(nc.psum_tensor("ps", [P, 8, 512], F32))
        h_rows = nc.dram_tensor("h_rows", [T + P, D], F32, kind="Internal").ap()
        acc = nc.dram_tensor("acc", [T + P, D], F32, kind="Internal").ap()

        x_landed = [sem(f"x_landed{t}") for t in range(TT)]
        w_in_landed = [sem(f"w_in_landed{k}") for k in range(DK)]
        small_landed, bias_landed = sem("small_landed"), sem("bias_landed")
        wqkv_landed, w_out_landed = sem("wqkv_landed"), sem("w_out_landed")
        consts, pool_step, act_step, dve_step = sem("consts"), sem("pool_step"), sem("act_step"), sem("dve_step")
        posf_ready, cols_turned, cols_ready = sem("posf_ready"), sem("cols_turned"), sem("cols_ready")
        xstd_ready, xn_ready, x_turned0 = sem("xstd_ready"), sem("xn_ready"), sem("x_turned0")
        hT_dve, hT_act = sem("hT_dve"), sem("hT_act")
        pair_ready, sg_ready, glu_done = sem("pair_ready"), sem("sg_ready"), sem("glu_done")
        ang_ready, trig_ready = sem("ang_ready"), sem("trig_ready")
        lat_ready, lat_sq, lat_done = sem("lat_ready"), sem("lat_sq"), sem("lat_done")
        krope_ready, krope_copied, lat_ss, lat_std_ready, lat_rs_ready = (
            sem("krope_ready"), sem("krope_copied"), sem("lat_ss"), sem("lat_std_ready"), sem("lat_rs_ready"))
        bias_turned, bias_ready = sem("bias_turned"), sem("bias_ready")
        rows_ready, rows_out, rowsq_ready, hss_ready, hstd_ready, headnorm = (
            sem("rows_ready"), sem("rows_out"), sem("rowsq_ready"), sem("hss_ready"), sem("hstd_ready"), sem("headnorm"))
        gained, roped, rows_turned, rowsT_out = sem("gained"), sem("roped"), sem("rows_turned"), sem("rowsT_out")
        conv_done, ln_mean, ln_xc, ln_sq, ln_var, ln_stdr = (
            sem("conv_done"), sem("ln_mean"), sem("ln_xc"), sem("ln_sq"), sem("ln_var"), sem("ln_stdr"))
        ln_norm, ln_sig, ln_silu, conv_sq, conv_ss, conv_std, conv_mix, c_rs_ready = (
            sem("ln_norm"), sem("ln_sig"), sem("ln_silu"), sem("conv_sq"), sem("conv_ss"), sem("conv_std"), sem("conv_mix"), sem("c_rs_ready"))
        s_ready, max_ready, exp_ready, pT_ready, pT_out, pv_done = (
            sem("s_ready"), sem("max_ready"), sem("exp_ready"), sem("pT_ready"), sem("pT_out"), sem("pv_done"))
        o_normed, a_ss_ready, o_turned, attn_mix, a_std_ready = (
            sem("o_normed"), sem("a_ss_ready"), sem("o_turned"), sem("attn_mix"), sem("a_std_ready"))
        out_ready, x1_ready, std1_ready, hn_ready, hn_turned, h2_act, h2_dve, log_ready, log_out = (
            sem("out_ready"), sem("x1_ready"), sem("std1_ready"), sem("hn_ready"), sem("hn_turned"),
            sem("h2_act"), sem("h2_dve"), sem("log_ready"), sem("log_out"))
        router_scaled = sem("router_scaled")
        stored = sem("stored")
        topd_ready, texp_ready, mask_ready, pos_ready, nt_ready, start_ready, mem_ready, fields_ready, tab_ready = (
            sem("topd_ready"), sem("texp_ready"), sem("mask_ready"), sem("pos_ready"), sem("nt_ready"),
            sem("start_ready"), sem("mem_ready"), sem("fields_ready"), sem("tab_ready"))
        landed = [sem(f"landed{c}") for c in range(CHUNKS)]
        used = [sem(f"used{c}") for c in range(CHUNKS)]
        hot_ready, slots_ready, slots_out, gathered = sem("hot_ready"), sem("slots_ready"), sem("slots_out"), sem("gathered")
        x_turned, xT_ready, gmin_ready, sig_ready, swiglu_done = (
            sem("x_turned"), sem("xT_ready"), sem("gmin_ready"), sem("sig_ready"), sem("swiglu_done"))
        yT_ready, y_turned, yrow_ready, hold_ready, scattered = (
            sem("yT_ready"), sem("y_turned"), sem("yrow_ready"), sem("hold_ready"), sem("scattered"))
        pool_go, moe_step, final = sem("pool_go"), sem("moe_step"), sem("final")

        N_SMALL = 14
        block = ctx.enter_context(nc.Block())

        def q_bank(t):
            return 6 if t % 2 == 0 else 2

        def kv_bank(t):
            return 0 if t % 2 == 0 else 4

        def unit_bank(u):
            return q_bank(u // 2) if u % 2 == 0 else kv_bank(u // 2)

        class Steps:

            def __init__(self, eng, s):
                self.eng, self.s, self.n = eng, s, 0

            def mark(self, ins):
                self.n += 1
                ins.then_inc(self.s, 1)
                return self.n

            def settle(self, ins):
                self.eng.wait_ge(self.s, self.mark(ins))

        def gu_src(e, c):
            a, kp = c // 4, c % 4
            return A["w_gate_up"][0, e, kp * 2 * P:(kp + 1) * 2 * P, :].rearrange(
                "(k p) (g a f) -> a p k g f", p=P, g=2, a=2)[a]

        @block.sync
        def _(sp):
            for t in range(TT):
                sp.dma_start(x[:, t, :], A["x"][0, t * P:(t + 1) * P, :]).then_inc(x_landed[t], 16)
            for k in range(DK):
                sp.dma_start(w_in[:, k, :], A["w_in"][0, k * P:(k + 1) * P, :]).then_inc(w_in_landed[k], 16)
            sp.dma_start(w_uq[:], A["w_uq"][0].rearrange("(j p) n -> p j n", p=P)).then_inc(wqkv_landed, 16)
            sp.dma_start(w_ukv[:], A["w_ukv"][0]).then_inc(wqkv_landed, 16)
            sp.dma_start(w_out[:], A["w_out"][0].rearrange("(k p) n -> p k n", p=P)).then_inc(w_out_landed, 16)

            def load_chunk(e, c):
                if c < GU_CHUNKS:
                    a, kp = c // 4, c % 4
                    for kk in range(2):
                        r0 = (kp * 2 + kk) * P
                        sp.dma_start(ring[c][:, kk], A["w_gate_up"][0, e, r0:r0 + P, :].rearrange(
                            "p (g a f) -> a p g f", g=2, a=2)[a]).then_inc(landed[c], 16)
                else:
                    r0 = (c - GU_CHUNKS) * 2 * P
                    sp.dma_start(ring[c][:], A["w_down"][0, e, r0:r0 + 2 * P, :].rearrange(
                        "(k p) n -> p k n", p=P)).then_inc(landed[c], 16)

            sp.wait_ge(s_ready, TT * H)
            sp.wait_ge(ln_silu, 1)
            sp.wait_ge(conv_ss, 1)
            for c in range(GU_CHUNKS):
                load_chunk(0, c)
            for t in range(TT):
                sp.wait_ge(x1_ready, t + 1)
                sp.dma_start(acc[t * P:(t + 1) * P, :], x[:, t, :]).then_inc(stored, 16)
                if t == 0:
                    sp.dma_start(acc[T:T + P, :], x[:, t, :]).then_inc(stored, 16)
                sp.wait_ge(hn_ready, t + 1)
                sp.dma_start(h_rows[t * P:(t + 1) * P, :], hn[:, t, :]).then_inc(stored, 16)
                if t == 0:
                    sp.dma_start(h_rows[T:T + P, :], hn[:, t, :]).then_inc(stored, 16)
            sp.wait_ge(out_ready, TT)
            for c in range(GU_CHUNKS, CHUNKS):
                load_chunk(0, c)
            sp.wait_ge(tab_ready, 1)
            with sp.Fori(1, E) as e:
                before = sp.value_load(tab[0:1, bass.ds(e + TAB_T, 1)], min_val=1, max_val=MAX_TILES)
                for c in range(CHUNKS):
                    sp.wait_ge(used[c], before)
                    load_chunk(e, c)
            tiles = sp.value_load(tab[0:1, TAB_T + E:TAB_T + E + 1], min_val=E, max_val=MAX_TILES)
            sp.wait_ge(scattered, tiles * 16 + 16)
            sp.dma_start(A["out"][0], acc[0:T, :]).then_inc(final, 16)
            sp.wait_ge(final, 16)

        @block.gpsimd
        def _(pool):
            st = Steps(pool, pool_step)
            g = nc.gpsimd
            g.memset(ident[:], 0.0).then_inc(pool_step, 1)
            g.memset(tri[:], 1.0).then_inc(pool_step, 1)
            g.memset(ones[:], 1.0).then_inc(consts, 1)
            g.memset(inv_c[:], 1.0 / CONV).then_inc(consts, 1)
            st.n = 2
            pool.wait_ge(pool_step, 2)
            g.affine_select(out=ident[:], in_=ident[:], compare_op=ALU.not_equal, fill=1.0, base=0,
                            pattern=[[-1, P]], channel_multiplier=1).then_inc(consts, 1)
            g.affine_select(out=tri[:], in_=tri[:], compare_op=ALU.is_gt, fill=0.0, base=0,
                            pattern=[[1, P]], channel_multiplier=-1).then_inc(consts, 1)
            g.memset(eps[:], EPS).then_inc(consts, 1)
            freq = np.float32(1) / np.float32(10000) ** (np.arange(0, ROPE, 2, dtype=np.float32) / np.float32(ROPE))
            for n in range(ROPE // 2):
                g.memset(inv_freq[:, n:n + 1], float(freq[n])).then_inc(consts, 1)
            g.memset(ypad[:, :, 0:PAD], 0.0).then_inc(consts, 1)
            g.iota(iota_s[:], [[1, T]], base=0, channel_multiplier=0,
                   allow_small_or_imprecise_dtypes=True).then_inc(consts, 1)
            g.iota(slot_row[:], [[0, 1]], base=T, channel_multiplier=1,
                   allow_small_or_imprecise_dtypes=True).then_inc(consts, 1)
            g.iota(eidx[:], [[0, 1]], base=0, channel_multiplier=1,
                   allow_small_or_imprecise_dtypes=True).then_inc(consts, 1)
            g.iota(tokv[:, :, 0], [[P, TT]], base=0, channel_multiplier=1,
                   allow_small_or_imprecise_dtypes=True).then_inc(consts, 1)
            g.memset(tokv[:, :, 1], 1.0).then_inc(consts, 1)
            g.iota(idx_hold[:], [[0, 1]], base=T, channel_multiplier=1).then_inc(consts, 1)
            g.memset(gate_hold[:], 0.0).then_inc(consts, 1)
            pool.wait_ge(small_landed, 16 * N_SMALL)
            for u in range(2 * TT):
                pool.wait_ge(headnorm, u + 1)
                r = rows[u % 4]
                g.tensor_tensor(r[:], r[:], qk_gain[:, u % 2, :].unsqueeze(1).broadcast_to([P, H, HD]),
                                ALU.mult).then_inc(gained, 1)
            pool.wait_ge(tab_ready, 1)
            n_tiles = pool.value_load(tab[0:1, TAB_T + E:TAB_T + E + 1], min_val=E, max_val=MAX_TILES)
            pool.wait_ge(stored, 16 * 2 * (TT + 1))

            def gather():
                pool.indirect_dma_start(out=xg[:], out_offset=None, in_=h_rows,
                                        in_offset=bass.IndirectOffsetOnAxis(ap=idx_next[:, 0:1], axis=0),
                                        bounds_check=T + P - 1).then_inc(gathered, 16)

            def scatter():
                pool.indirect_dma_start(out=acc, out_offset=bass.IndirectOffsetOnAxis(ap=idx_hold[:, 0:1], axis=0),
                                        in_=yrow[:], in_offset=None, bounds_check=T + P - 1,
                                        compute_op=ALU.add).then_inc(scattered, 16)

            pool.wait_ge(slots_out, 1)
            gather()
            with pool.Fori(0, MAX_TILES) as i:
                with pool.If(i < n_tiles):
                    pool.wait_ge(slots_out, i + 2)
                    pool.sem_inc(pool_go, 1)
                    pool.wait_ge(x_turned, i + 1)
                    pool.sem_inc(pool_go, 1)
                    gather()
                    pool.wait_ge(yrow_ready, i + 1)
                    pool.sem_inc(pool_go, 1)
                    scatter()
            pool.wait_ge(yrow_ready, n_tiles + 1)
            pool.sem_inc(pool_go, 1)
            scatter()

        @block.tensor
        def _(pe):
            mm, tr = nc.tensor.matmul, nc.tensor.transpose
            pe.wait_ge(consts, 13 + ROPE // 2)
            pe.wait_ge(small_landed, 16 * N_SMALL)
            tr(ps[:, 7, 0:V_W], vec_rows[:], ident[0:V_W, 0:V_W])
            tr(ps[:, 7, V_W:V_POS], dw_rows[:], ident[0:TAPS * CC, 0:TAPS * CC])
            pe.wait_ge(posf_ready, 1)
            tr(ps[:, 7, V_POS:V_ALL], pos_f[:], ident[0:TT, 0:TT]).then_inc(cols_turned, 1)
            pe.wait_ge(cols_ready, 1)
            for t in range(TT):
                pe.wait_ge(xn_ready, t + 1)
                for k in range(DK):
                    last = tr(ps[:, k, t * P:(t + 1) * P], xn[:, t, k * P:(k + 1) * P], ident[:])
            last.then_inc(x_turned0, 1)

            pe.wait_ge(hT_dve, 4)
            pe.wait_ge(hT_act, 4)
            conv_cols = [c for n in range(CC) for c in (COL_A + n * P, COL_G + n * P)]
            for k in range(DK):
                pe.wait_ge(w_in_landed[k], 16)
                for b in range(4):
                    last = mm(ps[:, b, :], w_in[:, k, conv_cols[b]:conv_cols[b] + P], hT[:, k, :],
                              start=(k == 0), stop=(k == DK - 1))
            last.then_inc(pair_ready, 2)
            for b in range(4, 8):
                for k in range(DK):
                    last = mm(ps[:, b, :], w_in[:, k, conv_cols[b]:conv_cols[b] + P], hT[:, k, :],
                              start=(k == 0), stop=(k == DK - 1))
                if b % 2:
                    last.then_inc(pair_ready, 1)
            pe.wait_ge(glu_done, 2)
            for j in range(4):
                for k in range(DK):
                    last = mm(ps[:, j, :], w_in[:, k, j * P:(j + 1) * P], hT[:, k, :],
                              start=(k == 0), stop=(k == DK - 1))
                last.then_inc(lat_ready, 1)
            pe.wait_ge(glu_done, 3)
            for t in range(TT):
                for k in range(DK):
                    last = mm(ps[:, 4, t * ROPE:(t + 1) * ROPE], hT[:, k, t * P:(t + 1) * P],
                              w_in[:, k, COL_ROPE:COL_A], start=(k == 0), stop=(k == DK - 1))
            last.then_inc(krope_ready, 1)
            pe.wait_ge(lat_sq, 4)
            for t in range(TT):
                for j in range(QJ):
                    mm(ps[:, 5, t:t + 1], latsq[:, j, t * P:(t + 1) * P], ones[:, 0:1], start=(j == 0), stop=(j == QJ - 1))
                last = mm(ps[:, 5, 4 + t:5 + t], latsq[:, 3, t * P:(t + 1) * P], ones[:, 0:1], start=True, stop=True)
            last.then_inc(lat_ss, 1)
            pe.wait_ge(glu_done, 4)
            pe.wait_ge(bias_landed, 48)
            for n in range(4):
                tr(ps[:, 7, n * P:(n + 1) * P], bgu_rows[:, n, :], ident[:])
            for n in range(2):
                last = tr(ps[:, 6, n * P:(n + 1) * P], bdn_rows[:, n, :], ident[:])
            last.then_inc(bias_turned, 1)

            def up_project(t):
                for half in range(2):
                    for j in range(QJ):
                        last = mm(ps[:, q_bank(t) + half, 0:Q_RANK], latT[:, j, t * P:(t + 1) * P],
                                  w_uq[:, j, half * Q_RANK:(half + 1) * Q_RANK], start=(j == 0), stop=(j == QJ - 1))
                last.then_inc(rows_ready, 1)
                for half in range(2):
                    last = mm(ps[:, kv_bank(t) + half, :], latT[:, 3, t * P:(t + 1) * P],
                              w_ukv[:, half * 512:(half + 1) * 512], start=True, stop=True)
                last.then_inc(rows_ready, 1)

            def turn_unit(u):
                pe.wait_ge(roped, u + 1)
                for h in range(H):
                    last = tr(ps[0:HD, unit_bank(u) + h // 4, (h % 4) * P:(h % 4 + 1) * P], rows[u % 4][:, h, :], ident[:])
                last.then_inc(rows_turned, 1)

            pe.wait_ge(wqkv_landed, 32)
            pe.wait_ge(lat_done, 4)
            pe.wait_ge(bias_ready, 1)
            up_project(0)
            pe.wait_ge(krope_copied, 1)
            pe.wait_ge(lat_std_ready, 1)
            up_project(1)
            pe.wait_ge(conv_done, 1)
            pe.wait_ge(rows_out, 2)
            for c in range(CC):
                last = mm(ps[:, 0, :], inv_c[:], cacc[:, c, :], start=(c == 0), stop=(c == CC - 1))
            last.then_inc(ln_mean, 1)
            pe.wait_ge(ln_sq, 1)
            for c in range(CC):
                last = mm(ps[:, 1, :], inv_c[:], lnsq[:, c, :], start=(c == 0), stop=(c == CC - 1))
            last.then_inc(ln_var, 1)
            pe.wait_ge(conv_sq, 1)
            for t in range(TT):
                for c in range(CC):
                    last = mm(ps[:, 1, t:t + 1], lnsq[:, c, t * P:(t + 1) * P], ones[:, 0:1], start=(c == 0), stop=(c == CC - 1))
            last.then_inc(conv_ss, 1)
            turn_unit(0)
            turn_unit(1)
            pe.wait_ge(rowsT_out, 2)
            pe.wait_ge(conv_std, 1)
            up_project(2)
            turn_unit(2)
            turn_unit(3)
            pe.wait_ge(rowsT_out, 4)
            up_project(3)
            for u in range(4, 8):
                turn_unit(u)

            pe.wait_ge(rowsT_out, 8)

            def scores(s):
                qb, h = s // H, s % H
                if s >= 2:
                    pe.wait_ge(exp_ready, s - 1)
                mm(ps[:, s % 2, 0:(qb + 1) * P], qT[:, h, qb * P:(qb + 1) * P], kT[:, h, 0:(qb + 1) * P],
                   start=True, stop=True).then_inc(s_ready, 1)

            def turn_probs(s):
                qb = s // H
                pe.wait_ge(exp_ready, s + 1)
                if s >= 2:
                    pe.wait_ge(pT_out, s - 1)
                for n in range(qb + 1):
                    last = tr(ps[:, 2 + s % 2, n * P:(n + 1) * P], probs[:, s % 2, n * P:(n + 1) * P], ident[:])
                last.then_inc(pT_ready, 1)

            def weigh_values(s):
                qb, h = s // H, s % H
                pe.wait_ge(pT_out, s + 1)
                if h == 0 and qb >= 2:
                    pe.wait_ge(o_normed, qb - 1)
                for n in range(qb + 1):
                    last = mm(ps[:, 4 + qb % 2, h * VD:(h + 1) * VD], probsT[:, s % 2, n, :],
                              vrow[:, n, h * VD:(h + 1) * VD], start=(n == 0), stop=(n == qb))
                last.then_inc(pv_done, 1)

            def turn_attention(qb):
                pe.wait_ge(o_normed, qb + 1)
                if qb >= 2:
                    pe.wait_ge(attn_mix, qb - 1)
                for n in range(4):
                    last = tr(ps[:, 6 + qb % 2, n * P:(n + 1) * P], attn_row[:, qb % 2, n * P:(n + 1) * P], ident[:])
                last.then_inc(o_turned, 1)

            for s in range(TT * H + 6):
                if s < TT * H:
                    scores(s)
                if 1 <= s <= TT * H:
                    turn_probs(s - 1)
                if 2 <= s <= TT * H + 1:
                    weigh_values(s - 2)
                if s >= 13 and (s - 13) % H == 0:
                    turn_attention((s - 13) // H)

            def project_out(t):
                b = 4 * (t % 2)
                for part in range(2):
                    for half in range(2):
                        for k in range(4):
                            last = mm(ps[:, b + 2 * part + half, :], mixT[:, part * 4 + k, t * P:(t + 1) * P],
                                      w_out[:, part * 4 + k, half * 512:(half + 1) * 512], start=(k == 0), stop=(k == 3))
                last.then_inc(out_ready, 1)

            def route(t):
                b = 4 * (t % 2)
                pe.wait_ge(hn_ready, t + 1)
                for k in range(DK):
                    last = tr(ps[:, b + k // 4, (k % 4) * P:(k % 4 + 1) * P], hn[:, t, k * P:(k + 1) * P], ident[:])
                last.then_inc(hn_turned, 1)
                pe.wait_ge(h2_act, t + 1)
                pe.wait_ge(h2_dve, t + 1)
                for k in range(DK):
                    last = mm(ps[:, b + 2, 0:E], h2T[:, t % 2, k, :], router[:, k, :], start=(k == 0), stop=(k == DK - 1))
                last.then_inc(log_ready, 1)

            pe.wait_ge(w_out_landed, 16)
            pe.wait_ge(conv_mix, 4)
            pe.wait_ge(attn_mix, TT)
            pe.wait_ge(router_scaled, 1)
            project_out(0)
            project_out(1)
            route(0)
            pe.wait_ge(log_out, 1)
            project_out(2)
            route(1)
            pe.wait_ge(log_out, 2)
            project_out(3)
            route(2)
            route(3)

            pe.wait_ge(mask_ready, 1)
            for t in range(TT):
                for n in range(t):
                    mm(ps[:, 0, t * E:(t + 1) * E], ones[:], mask[:, n, :], start=(n == 0), stop=False)
                mm(ps[:, 0, t * E:(t + 1) * E], tri[:], mask[:, t, :], start=(t == 0), stop=True)
            for t in range(TT):
                last = mm(ps[0:E, 1, 0:1], mask[:, t, :], ones[:, 0:1], start=(t == 0), stop=(t == TT - 1))
            last.then_inc(pos_ready, 1)
            pe.wait_ge(nt_ready, 1)
            mm(ps[0:E, 1, 4:5], tri[0:E, 0:E], cnt[:, 1:2], start=True, stop=True)
            mm(ps[0:1, 1, 8:8 + E + 1], cnt[:, 1:2], tri[0:E, 0:E + 1], start=True, stop=True).then_inc(start_ready, 1)
            pe.wait_ge(mem_ready, 1)
            mm(ps[0:1, 2, TAB_E:TAB_E + TAB], eidx[:], member[:], start=True, stop=True)
            mm(ps[0:1, 2, TAB_J:TAB_J + TAB], ones[0:E, 0:1], memj[:], start=True, stop=True)
            mm(ps[0:1, 2, TAB_N:TAB_N + TAB], ones[0:E, 0:1], memn[:], start=True, stop=True).then_inc(fields_ready, 1)

            def fill_slots():
                for t in range(TT):
                    last = mm(ps[:, 4, 0:3], onehot[:, t, :], tokv[:, t, :], start=(t == 0), stop=(t == TT - 1))
                last.then_inc(slots_ready, 1)

            def turn_x():
                for k in range(DK):
                    last = tr(ps[:, 6 + k // 4, (k % 4) * P:(k % 4 + 1) * P], xg[:, k * P:(k + 1) * P], ident[:])
                last.then_inc(x_turned, 1)

            def turn_y():
                for k in range(DK):
                    last = tr(ps[:, 6 + k // 4, (k % 4) * P:(k % 4 + 1) * P], yT[:, k, :], ident[:])
                last.then_inc(y_turned, 1)

            pe.wait_ge(tab_ready, 1)
            n_tiles = pe.value_load(tab[0:1, TAB_T + E:TAB_T + E + 1], min_val=E, max_val=MAX_TILES)
            pe.wait_ge(hot_ready, 1)
            fill_slots()
            pe.wait_ge(gathered, 16)
            turn_x()

            def products(i, e, n):
                def gate_up(a):
                    for kp in range(4):
                        c = a * 4 + kp
                        pe.wait_ge(landed[c], e * 32 + 32)
                        for kk in range(2):
                            k = kp * 2 + kk
                            for gu in range(2):
                                for f in range(4):
                                    last = mm(ps[:, 2 * a + gu, f * P:f * P + n], ring[c][:, kk, gu, f * P:(f + 1) * P],
                                              xT[:, k, 0:n], start=(k == 0 and f == 0), stop=(k == DK - 1),
                                              skip_group_check=True)
                        last.then_inc(used[c], 1)

                def down(lo):
                    for c in range(lo, lo + 2):
                        pe.wait_ge(landed[GU_CHUNKS + c], e * 16 + 16)
                        for kk in range(2):
                            k = c * 2 + kk
                            for d in range(DK):
                                last = mm(ps[:, 4 + d // 4, (d % 4) * P:(d % 4) * P + n],
                                          ring[GU_CHUNKS + c][:, kk, d * P:(d + 1) * P], act_T[:, k, 0:n],
                                          start=(k == 0 and d % 4 == 0), stop=(k == DK - 1), skip_group_check=True)
                        last.then_inc(used[GU_CHUNKS + c], 1)

                pe.wait_ge(xT_ready, i + 1)
                gate_up(0)
                pe.wait_ge(yT_ready, i + 1)
                turn_y()
                pe.wait_ge(hot_ready, i + 2)
                fill_slots()
                gate_up(1)
                pe.wait_ge(slots_out, i + 2)
                pe.wait_ge(swiglu_done, i * 2 + 1)
                down(0)
                pe.wait_ge(gathered, i * 16 + 32)
                pe.wait_ge(yrow_ready, i + 1)
                turn_x()
                pe.wait_ge(swiglu_done, i * 2 + 2)
                down(2)

            with pe.Fori(0, MAX_TILES) as i:
                with pe.If(i < n_tiles):
                    e = pe.value_load(tab[0:1, bass.ds(i + TAB_E, 1)], min_val=0, max_val=E - 1)
                    n = pe.value_load(tab[0:1, bass.ds(i + TAB_N, 1)], min_val=0, max_val=T)
                    with pe.If(n < 97):
                        products(i, e, 96)
                    with pe.Else():
                        products(i, e, 128)
            pe.wait_ge(yT_ready, n_tiles + 1)
            turn_y()

        @block.scalar
        def _(act):
            st = Steps(act, act_step)
            f = nc.scalar.activation

            def load(dst, src, s=small_landed):
                act.dma_start(dst, src).then_inc(s, 16)

            for col, name in ((V_MIX, "norm_mix_g"), (V_QL, "q_latent_g"), (V_KL, "kv_latent_g"), (V_DWB, "conv_dw_b"),
                              (V_LNG, "conv_ln_g"), (V_LNB, "conv_ln_b"), (V_AG, "attn_out_g"), (V_CG, "conv_out_g"),
                              (V_FG, "norm_ffn_g")):
                v = A[name][0].rearrange("(r c) -> r c", c=P)
                load(vec_rows[col:col + v.shape[0], :], v)
            load(dw_rows[:], A["conv_dw_w"][0].rearrange("j (c p) -> (j c) p", p=P))
            load(pos_i[:], A["positions"][0].rearrange("(t p) -> t p", p=P))
            load(qk_gain[:, 0, :], A["q_head_g"].broadcast_to([P, HD]))
            load(qk_gain[:, 1, :], A["k_head_g"].broadcast_to([P, HD]))
            load(router_bias[:], A["router_b"].broadcast_to([P, E]))
            load(router[:], A["router_w"][0].rearrange("(k p) e -> p k e", p=P), bias_landed)
            load(bgu_rows[:], A["b_gate_up"][0].rearrange("e (f c) -> (e f) c", c=P).rearrange("(n p) c -> p n c", p=P), bias_landed)
            load(bdn_rows[:], A["b_down"][0].rearrange("e (f c) -> (e f) c", c=P).rearrange("(n p) c -> p n c", p=P), bias_landed)

            act.wait_ge(consts, 13 + ROPE // 2)
            for t in range(TT):
                act.wait_ge(x_landed[t], 16)
                st.settle(f(xn[:, t, :], x[:, t, :], ACT.Square, accum_out=ssx[:, t:t + 1]))
                f(stdx[:, t:t + 1], ssx[:, t:t + 1], ACT.Sqrt, bias=eps[:, 0:1], scale=1.0 / D).then_inc(xstd_ready, 1)
            act.wait_ge(cols_ready, 1)
            act.wait_ge(x_turned0, 1)
            for k in range(1, DK, 2):
                f(hT[:, k, :], ps[:, k, :], ACT.Copy, scale=vcol[:, V_MIX + k:V_MIX + k + 1]).then_inc(hT_act, 1)
            act.wait_ge(ang_ready, 1)
            f(sin_[:], red[:, 0], ACT.Sin).then_inc(trig_ready, 1)
            f(cosd[:, :, 0, :], red[:, 1], ACT.Sin).then_inc(trig_ready, 1)
            f(cosd[:, :, 1, :], red[:, 1], ACT.Sin).then_inc(trig_ready, 1)
            for c in range(CC):
                act.wait_ge(pair_ready, max(c + 1, 2))
                if c >= 2:
                    act.wait_ge(glu_done, c - 1)
                f(sgl[:, c % 2, :], ps[:, 2 * c + 1, :], ACT.Sigmoid).then_inc(sg_ready, 1)
            for j in range(4):
                act.wait_ge(lat_ready, j + 1)
                f(latsq[:, j, :], ps[:, j, :], ACT.Square).then_inc(lat_sq, 1)
                f(latT[:, j, :], ps[:, j, :], ACT.Copy, scale=vcol[:, V_QL + j:V_QL + j + 1]).then_inc(lat_done, 1)
            act.wait_ge(krope_ready, 1)
            f(krope[:].rearrange("p t r -> p (t r)"), ps[:, 4, 0:TT * ROPE], ACT.Copy).then_inc(krope_copied, 1)
            act.wait_ge(lat_ss, 1)
            f(lat_std[:, 0:4], ps[:, 5, 0:4], ACT.Sqrt, bias=eps[:, 0:1], scale=1.0 / Q_RANK)
            f(lat_std[:, 4:8], ps[:, 5, 4:8], ACT.Sqrt, bias=eps[:, 0:1], scale=1.0 / KV_RANK).then_inc(lat_std_ready, 1)
            act.wait_ge(bias_turned, 1)
            f(biasT[:, :, 0:16], ps[:, 7, :].rearrange("p (e f) -> p e f", f=16), ACT.Copy)
            f(biasT[:, :, 16:24], ps[:, 6, 0:256].rearrange("p (e f) -> p e f", f=8), ACT.Copy).then_inc(bias_ready, 1)

            def rows_to_sbuf(u):
                t, b, r = u // 2, unit_bank(u), rows[u % 4]
                act.wait_ge(rows_ready, u + 1)
                if u >= 4:
                    act.wait_ge(rows_turned, u - 3)
                if u % 2 == 0:
                    for half in range(2):
                        last = f(r[:, half * 4:half * 4 + 4, :], ps[:, b + half, 0:Q_RANK].rearrange("p (h d) -> p h d", d=HD),
                                 ACT.Copy, scale=lat_rs[:, t:t + 1])
                else:
                    for half in range(2):
                        src = ps[:, b + half, :].rearrange("p (h d) -> p h d", d=NOPE + VD)
                        f(r[:, half * 4:half * 4 + 4, 0:NOPE], src[:, :, 0:NOPE], ACT.Copy, scale=lat_rs[:, 4 + t:5 + t])
                        f(vrow[:, t, half * 256:(half + 1) * 256].rearrange("p (h d) -> p h d", d=VD), src[:, :, NOPE:],
                          ACT.Copy, scale=lat_rs[:, 4 + t:5 + t])
                    last = f(r[:, :, NOPE:], krope[:, t, :].unsqueeze(1).broadcast_to([P, H, ROPE]), ACT.Copy)
                last.then_inc(rows_out, 1)

            act.wait_ge(lat_rs_ready, 1)
            for u in range(4):
                rows_to_sbuf(u)
            act.wait_ge(ln_xc, 1)
            f(lnsq[:], cacc[:], ACT.Square).then_inc(ln_sq, 1)
            act.wait_ge(ln_var, 1)
            f(ln_std[:], ps[:, 1, :], ACT.Sqrt, bias=eps[:, 0:1]).then_inc(ln_stdr, 1)
            act.wait_ge(ln_norm, 1)
            for c in range(CC):
                last = f(cacc[:, c, :], cacc[:, c, :], ACT.Identity, bias=vcol[:, V_LNB + c:V_LNB + c + 1],
                         scale=vcol[:, V_LNG + c:V_LNG + c + 1])
            st.settle(last)
            f(lnsq[:], cacc[:], ACT.Sigmoid).then_inc(ln_sig, 1)
            act.wait_ge(ln_silu, 1)
            f(lnsq[:], cacc[:], ACT.Square).then_inc(conv_sq, 1)
            for c in range(CC):
                f(mixT[:, 4 + c, :], cacc[:, c, :], ACT.Copy, scale=vcol[:, V_CG + c:V_CG + c + 1]).then_inc(conv_mix, 1)
            act.wait_ge(conv_ss, 1)
            f(css[:], ps[:, 1, 0:TT], ACT.Sqrt, bias=eps[:, 0:1], scale=1.0 / CONV).then_inc(conv_std, 1)
            for u in range(2 * TT + 2):
                if 4 <= u < 8:
                    rows_to_sbuf(u)
                if u < 8:
                    if u >= 4:
                        act.wait_ge(rows_out, u + 1)
                    if u >= 2:
                        act.wait_ge(hss_ready, u - 1)
                    f(rowsq[:, u % 2, :], rows[u % 4][:].rearrange("p h d -> p (h d)"), ACT.Square).then_inc(rowsq_ready, 1)
                if 1 <= u <= 8:
                    act.wait_ge(hss_ready, u)
                    f(hstd[:, u - 1, :], hss[:, u - 1, :], ACT.Sqrt, bias=eps[:, 0:1], scale=1.0 / HD).then_inc(hstd_ready, 1)
                if u >= 2:
                    w = u - 2
                    act.wait_ge(rows_turned, w + 1)
                    dst = qT if w % 2 == 0 else kT
                    for half in range(2):
                        last = f(dst[:, half * 4:half * 4 + 4, (w // 2) * P:(w // 2 + 1) * P],
                                 ps[0:HD, unit_bank(w) + half, :].rearrange("p (h t) -> p h t", t=P), ACT.Copy)
                    last.then_inc(rowsT_out, 1)
            for s in range(TT * H + 1):
                if s < TT * H:
                    act.wait_ge(max_ready, s + 1)
                    if s >= 2:
                        act.wait_ge(pT_ready, s - 1)
                    w = (s // H + 1) * P
                    f(probs[:, s % 2, 0:w], ps[:, s % 2, 0:w], ACT.Exp, bias=nmx[:, s:s + 1], scale=SCALE,
                      accum_out=den[:, s // H, s % H:s % H + 1]).then_inc(exp_ready, 1)
                if s >= 1:
                    z = s - 1
                    act.wait_ge(pT_ready, z + 1)
                    if z >= 2:
                        act.wait_ge(pv_done, z - 1)
                    w = z // H + 1
                    f(probsT[:, z % 2, 0:w, :], ps[:, 2 + z % 2, 0:w * P].rearrange("p (n q) -> p n q", q=P),
                      ACT.Copy).then_inc(pT_out, 1)
            act.wait_ge(a_ss_ready, TT)
            f(astd[:], ass_[:], ACT.Sqrt, bias=eps[:, 0:1], scale=1.0 / (H * VD)).then_inc(a_std_ready, 1)
            for t in range(TT):
                act.wait_ge(x1_ready, t + 1)
                st.settle(f(hn[:, t, :], x[:, t, :], ACT.Square, accum_out=ss1[:, t:t + 1]))
                f(std1[:, t:t + 1], ss1[:, t:t + 1], ACT.Sqrt, bias=eps[:, 0:1], scale=1.0 / D).then_inc(std1_ready, 1)
                act.wait_ge(hn_turned, t + 1)
                if t >= 2:
                    act.wait_ge(log_ready, t - 1)
                f(h2T[:, t % 2, 0:4, :], ps[:, 4 * (t % 2), :].rearrange("p (k q) -> p k q", q=P), ACT.Copy).then_inc(h2_act, 1)
            act.wait_ge(topd_ready, 1)
            f(tg[:], tg[:], ACT.Exp).then_inc(texp_ready, 1)

            def rows_of_y():
                for half in range(2):
                    last = f(yrow[:, half * 512:(half + 1) * 512], ps[:, 6 + half, :], ACT.Copy, scale=gate_hold[:, 0:1])
                last.then_inc(yrow_ready, 1)

            act.wait_ge(tab_ready, 1)
            n_tiles = act.value_load(tab[0:1, TAB_T + E:TAB_T + E + 1], min_val=E, max_val=MAX_TILES)
            with act.Fori(0, MAX_TILES) as i:
                with act.If(i < n_tiles):
                    act.wait_ge(hold_ready, i + 1)
                    act.wait_ge(y_turned, i + 1)
                    rows_of_y()
                    for a in range(2):
                        act.wait_ge(gmin_ready, i * 2 + (a + 1))
                        f(g_sig[:], g_in[:], ACT.Sigmoid, scale=ALPHA).then_inc(sig_ready, 1)
            act.wait_ge(hold_ready, n_tiles + 1)
            act.wait_ge(y_turned, n_tiles + 1)
            rows_of_y()

        @block.vector
        def _(dve):
            v = nc.vector
            st = Steps(dve, dve_step)

            dve.wait_ge(small_landed, 16 * N_SMALL)
            v.tensor_copy(pos_f[:], pos_i[:]).then_inc(posf_ready, 1)
            dve.wait_ge(cols_turned, 1)
            v.tensor_copy(vcol[:], ps[:, 7, 0:V_ALL]).then_inc(cols_ready, 1)
            dve.wait_ge(cols_ready, 1)
            for t in range(TT):
                dve.wait_ge(xstd_ready, t + 1)
                st.settle(v.reciprocal(rsx[:, t:t + 1], stdx[:, t:t + 1]))
                v.tensor_scalar(xn[:, t, :], x[:, t, :], rsx[:, t:t + 1], None, ALU.mult).then_inc(xn_ready, 1)
            dve.wait_ge(x_turned0, 1)
            for k in range(0, DK, 2):
                v.tensor_scalar(hT[:, k, :], ps[:, k, :], vcol[:, V_MIX + k:V_MIX + k + 1], None, ALU.mult).then_inc(hT_dve, 1)

            dve.wait_ge(consts, 13 + ROPE // 2)
            st.settle(v.tensor_tensor(ang[:], vcol[:, V_POS:V_ALL].unsqueeze(2).broadcast_to([P, TT, 16]),
                                      inv_freq[:].unsqueeze(1).broadcast_to([P, TT, 16]), ALU.mult))
            for c in range(2):
                n_, r_ = turns[:, c], red[:, c]
                st.settle(v.tensor_scalar(n_, ang[:], 1.0 / TWO_PI, 0.25 * c, ALU.mult, ALU.add))
                st.settle(v.tensor_scalar(n_, n_, ROUND, ROUND, ALU.add, ALU.subtract))
                st.settle(v.scalar_tensor_tensor(out=r_, in0=n_, scalar=-PI2_A, in1=ang[:], op0=ALU.mult, op1=ALU.add))
                st.settle(v.scalar_tensor_tensor(out=r_, in0=n_, scalar=-PI2_B, in1=r_, op0=ALU.mult, op1=ALU.add))
                st.settle(v.scalar_tensor_tensor(out=r_, in0=n_, scalar=-PI2_C, in1=r_, op0=ALU.mult, op1=ALU.add))
                st.settle(v.tensor_scalar(r_, r_, 0.5 * np.pi * c, PI_IN, ALU.add, ALU.min))
                last = v.tensor_scalar(r_, r_, -PI_IN, None, ALU.max)
                if c == 0:
                    st.settle(last)
            last.then_inc(ang_ready, 1)
            dve.wait_ge(trig_ready, 3)
            st.settle(v.tensor_scalar(nsin[:], sin_[:], -1.0, None, ALU.mult))
            dve.wait_ge(bias_landed, 48)
            v.tensor_tensor(router[:], router[:], vcol[:, V_FG:V_FG + DK].unsqueeze(2).broadcast_to([P, DK, E]),
                            ALU.mult).then_inc(router_scaled, 1)

            for pair in range(2):
                for c in (2 * pair, 2 * pair + 1):
                    dve.wait_ge(sg_ready, c + 1)
                    v.tensor_tensor(ypad[:, c, PAD:], ps[:, 2 * c, :], sgl[:, c % 2, :], ALU.mult).then_inc(glu_done, 1)
                dve.wait_ge(glu_done, 2 * pair + 2)
                before = {}
                for j in range(TAPS):
                    for c in (2 * pair, 2 * pair + 1):
                        w = vcol[:, V_W + j * CC + c:V_W + j * CC + c + 1]
                        if j == 0:
                            ins = v.tensor_scalar(cacc[:, c, :], ypad[:, c, 0:T], w, vcol[:, V_DWB + c:V_DWB + c + 1],
                                                  ALU.mult, ALU.add)
                        else:
                            dve.wait_ge(dve_step, before[c])
                            ins = v.scalar_tensor_tensor(out=cacc[:, c, :], in0=ypad[:, c, j:j + T], scalar=w,
                                                         in1=cacc[:, c, :], op0=ALU.mult, op1=ALU.add)
                        before[c] = st.mark(ins)
                dve.wait_ge(dve_step, st.n)
            dve.sem_inc(conv_done, 1)
            dve.wait_ge(lat_std_ready, 1)
            v.reciprocal(lat_rs[:], lat_std[:]).then_inc(lat_rs_ready, 1)

            dve.wait_ge(ln_mean, 1)
            v.tensor_tensor(cacc[:], cacc[:], ps[:, 0, :].unsqueeze(1).broadcast_to([P, CC, T]), ALU.subtract).then_inc(ln_xc, 1)
            dve.wait_ge(ln_stdr, 1)
            st.settle(v.reciprocal(ln_std[:], ln_std[:]))
            v.tensor_tensor(cacc[:], cacc[:], ln_std[:].unsqueeze(1).broadcast_to([P, CC, T]), ALU.mult).then_inc(ln_norm, 1)
            dve.wait_ge(ln_sig, 1)
            v.tensor_tensor(cacc[:], cacc[:], lnsq[:], ALU.mult).then_inc(ln_silu, 1)

            def head_norm(u):
                r = rows[u % 4]
                dve.wait_ge(rowsq_ready, u + 1)
                v.tensor_reduce(hss[:, u, :], rowsq[:, u % 2, :].rearrange("p (h d) -> p h d", d=HD), AX.X, ALU.add).then_inc(hss_ready, 1)
                dve.wait_ge(hstd_ready, u + 1)
                st.settle(v.reciprocal(hrs[:, u, :], hstd[:, u, :]))
                v.tensor_tensor(r[:], r[:], hrs[:, u, :].unsqueeze(2).broadcast_to([P, H, HD]), ALU.mult).then_inc(headnorm, 1)

            def rotate(u):
                t, r = u // 2, rows[u % 4]
                dve.wait_ge(gained, u + 1)
                if u:
                    dve.wait_ge(roped, u)
                v.tensor_tensor(rtmp[:, 0], r[:, :, NOPE:], cosd[:, t].rearrange("p a b -> p (a b)").unsqueeze(1).broadcast_to([P, H, ROPE]), ALU.mult)
                v.tensor_tensor(rtmp[:, 1, :, 0:16], r[:, :, NOPE + 16:], nsin[:, t, :].unsqueeze(1).broadcast_to([P, H, 16]), ALU.mult)
                st.settle(v.tensor_tensor(rtmp[:, 1, :, 16:32], r[:, :, NOPE:NOPE + 16], sin_[:, t, :].unsqueeze(1).broadcast_to([P, H, 16]), ALU.mult))
                v.tensor_tensor(r[:, :, NOPE:], rtmp[:, 0], rtmp[:, 1], ALU.add).then_inc(roped, 1)

            for u in range(2 * TT + 1):
                if u < 2 * TT:
                    head_norm(u)
                if u >= 1:
                    rotate(u - 1)
            dve.wait_ge(conv_std, 1)
            v.reciprocal(c_rs[:], css[:]).then_inc(c_rs_ready, 1)

            def row_max(s):
                w = (s // H + 1) * P
                dve.wait_ge(s_ready, s + 1)
                st.settle(v.memset(ps[0:CHUNK, s % 2, w - CHUNK:w], -1e30))
                st.settle(v.tensor_reduce(mx[:, s:s + 1], ps[:, s % 2, 0:w], AX.X, ALU.max))
                v.tensor_scalar(nmx[:, s:s + 1], mx[:, s:s + 1], -SCALE, None, ALU.mult).then_inc(max_ready, 1)

            def normalise(qb):
                dve.wait_ge(pv_done, (qb + 1) * H)
                st.settle(v.reciprocal(rden[:, qb, :], den[:, qb, :]))
                if qb >= 2:
                    dve.wait_ge(o_turned, qb - 1)
                v.tensor_tensor(attn_row[:, qb % 2, :].rearrange("p (h d) -> p h d", d=VD),
                                ps[:, 4 + qb % 2, :].rearrange("p (h d) -> p h d", d=VD),
                                rden[:, qb, :].unsqueeze(2).broadcast_to([P, H, VD]), ALU.mult).then_inc(o_normed, 1)
                dve.wait_ge(o_normed, qb + 1)
                v.tensor_tensor_reduce(out=ln_std[:], in0=attn_row[:, qb % 2, :], in1=attn_row[:, qb % 2, :], scale=1.0,
                                       scalar=0.0, op0=ALU.mult, op1=ALU.add, accum_out=ass_[:, qb:qb + 1]).then_inc(a_ss_ready, 1)

            def mix(qb):
                dve.wait_ge(o_turned, qb + 1)
                v.tensor_tensor(mixT[:, 0:4, qb * P:(qb + 1) * P], ps[:, 6 + qb % 2, :].rearrange("p (n q) -> p n q", q=P),
                                vcol[:, V_AG:V_AG + 4].unsqueeze(2).broadcast_to([P, 4, P]), ALU.mult).then_inc(attn_mix, 1)

            for s in range(TT * H + 7):
                if s < TT * H:
                    row_max(s)
                if s >= 11 and (s - 11) % H == 0:
                    normalise((s - 11) // H)
                if s >= 14 and (s - 14) % H == 0:
                    mix((s - 14) // H)

            dve.wait_ge(a_std_ready, 1)
            st.settle(v.reciprocal(a_rs[:], astd[:]))
            dve.wait_ge(c_rs_ready, 1)

            def residual(t):
                b = 4 * (t % 2)
                dve.wait_ge(out_ready, t + 1)
                for part, r in ((0, a_rs), (1, c_rs)):
                    for half in range(2):
                        xs = x[:, t, half * 512:(half + 1) * 512]
                        last = v.scalar_tensor_tensor(out=xs, in0=ps[:, b + 2 * part + half, :], scalar=r[:, t:t + 1],
                                                      in1=xs, op0=ALU.mult, op1=ALU.add)
                    if part == 0:
                        st.settle(last)
                last.then_inc(x1_ready, 1)

            def norm_ffn(t):
                dve.wait_ge(std1_ready, t + 1)
                st.settle(v.reciprocal(rs1[:, t:t + 1], std1[:, t:t + 1]))
                v.tensor_scalar(hn[:, t, :], x[:, t, :], rs1[:, t:t + 1], None, ALU.mult).then_inc(hn_ready, 1)

            def turned_out(t):
                dve.wait_ge(hn_turned, t + 1)
                if t >= 2:
                    dve.wait_ge(log_ready, t - 1)
                v.tensor_copy(h2T[:, t % 2, 4:8, :], ps[:, 4 * (t % 2) + 1, :].rearrange("p (k q) -> p k q", q=P)).then_inc(h2_dve, 1)

            def logits_out(t):
                dve.wait_ge(log_ready, t + 1)
                v.tensor_tensor(logits[:, t, :], ps[:, 4 * (t % 2) + 2, 0:E], router_bias[:], ALU.add).then_inc(log_out, 1)

            for t in range(TT):
                residual(t)
                norm_ffn(t)
                turned_out(t)
                logits_out(t)

            dve.wait_ge(log_out, TT)
            for t in range(TT):
                st.settle(v.max(top_v[:, t, :], logits[:, t, :]))
                st.settle(v.max_index(top_i[:, t, :], top_v[:, t, :], logits[:, t, :]))
            v.tensor_tensor(tg[:], top_v[:, :, 0:TOPK], top_v[:, :, 0:1].broadcast_to([P, TT, TOPK]), ALU.subtract).then_inc(topd_ready, 1)
            st.settle(v.tensor_copy(top_f[:], top_i[:, :, 0:TOPK]))
            st.settle(v.tensor_tensor(hot[:], iota_s[:, 0:E].unsqueeze(1).broadcast_to([P, 16, E]),
                                      top_f[:].rearrange("p t k -> p (t k)").unsqueeze(2).broadcast_to([P, 16, E]), ALU.is_equal))
            v.tensor_reduce(mask[:], hot[:].rearrange("p (t k) e -> p t e k", k=TOPK), AX.X, ALU.add).then_inc(mask_ready, 1)
            dve.wait_ge(texp_ready, 1)
            st.settle(v.tensor_reduce(tgs[:], tg[:], AX.X, ALU.add))
            st.settle(v.reciprocal(tgr[:], tgs[:]))
            st.settle(v.tensor_tensor(tg[:], tg[:], tgr[:].unsqueeze(2).broadcast_to([P, TT, TOPK]), ALU.mult))
            st.settle(v.tensor_tensor(hotg[:], hot[:], tg[:].rearrange("p t k -> p (t k)").unsqueeze(2).broadcast_to([P, 16, E]), ALU.mult))
            st.settle(v.tensor_reduce(gate[:], hotg[:].rearrange("p (t k) e -> p t e k", k=TOPK), AX.X, ALU.add))
            dve.wait_ge(pos_ready, 1)
            st.settle(v.tensor_copy(cnt[:, 0:1], ps[0:E, 1, 0:1]))
            st.settle(v.tensor_scalar(cnt[:, 1:2], cnt[:, 0:1], float(P), 1.0, ALU.is_gt, ALU.add))
            st.settle(v.scalar_tensor_tensor(out=cnt[:, 1:2], in0=cnt[:, 0:1], scalar=2.0 * P, in1=cnt[:, 1:2], op0=ALU.is_gt, op1=ALU.add))
            v.scalar_tensor_tensor(out=cnt[:, 1:2], in0=cnt[:, 0:1], scalar=3.0 * P, in1=cnt[:, 1:2], op0=ALU.is_gt, op1=ALU.add).then_inc(nt_ready, 1)
            st.settle(v.scalar_tensor_tensor(out=posm[:].rearrange("p t e -> p (t e)"), in0=ps[:, 0, 0:TT * E], scalar=NONE,
                                             in1=mask[:].rearrange("p t e -> p (t e)"), op0=ALU.add, op1=ALU.mult))
            st.settle(v.tensor_scalar(posm[:], posm[:], NONE, None, ALU.subtract))
            dve.wait_ge(start_ready, 1)
            st.settle(v.tensor_copy(cnt[:, 2:3], ps[0:E, 1, 4:5]))
            st.settle(v.tensor_tensor(cnt[:, 3:4], cnt[:, 2:3], cnt[:, 1:2], ALU.add))
            it = iota_s[0:E, 0:TAB]
            st.settle(v.tensor_scalar(memj[:], it, cnt[:, 2:3], None, ALU.is_ge))
            st.settle(v.scalar_tensor_tensor(out=member[:], in0=it, scalar=cnt[:, 3:4], in1=memj[:], op0=ALU.is_lt, op1=ALU.mult))
            st.settle(v.scalar_tensor_tensor(out=memj[:], in0=it, scalar=cnt[:, 2:3], in1=member[:], op0=ALU.subtract, op1=ALU.mult))
            st.settle(v.tensor_scalar(memn[:], memj[:], -float(P), cnt[:, 0:1], ALU.mult, ALU.add))
            v.tensor_tensor(memn[:], memn[:], member[:], ALU.mult).then_inc(mem_ready, 1)
            dve.wait_ge(fields_ready, 1)
            v.tensor_copy(tab[0:1, 0:TAB_T], ps[0:1, 2, 0:TAB_T])
            st.settle(v.tensor_copy(tab[0:1, TAB_T:TAB_T + E + 1], ps[0:1, 1, 8:8 + E + 1]))
            st.settle(v.memset(yT[:], 0.0))
            dve.sem_inc(tab_ready, 1)
            v.memset(ps[:, 0:4, :], 0.0)
            st.settle(v.memset(ps[:, 5, :], 0.0))

            def slots_of(tile, steps):
                e = dve.value_load(tab[0:1, bass.ds(tile + TAB_E, 1)], min_val=0, max_val=E - 1)
                j = dve.value_load(tab[0:1, bass.ds(tile + TAB_J, 1)], min_val=0, max_val=3)
                v.tensor_tensor(onehot[:], iota_s[:, bass.ds(j * P, P)].unsqueeze(1).broadcast_to([P, TT, P]),
                                posm[:, :, bass.ds(e, 1)].broadcast_to([P, TT, P]), ALU.is_equal)
                v.tensor_copy(tokv[:, :, 2:3], gate[:, :, bass.ds(e, 1)]).then_inc(hot_ready, 1)

            def slots_to_sbuf(steps):
                v.tensor_copy(gate_next[:], ps[:, 4, 2:3])
                steps(v.tensor_scalar(slot_f[:, 0:1], ps[:, 4, 1:2], -1.0, 1.0, ALU.mult, ALU.add))
                steps(v.scalar_tensor_tensor(out=slot_f[:, 1:2], in0=slot_f[:, 0:1], scalar=slot_row[:, 0:1],
                                             in1=ps[:, 4, 0:1], op0=ALU.mult, op1=ALU.add))
                v.tensor_copy(idx_next[:], slot_f[:, 1:2]).then_inc(slots_out, 1)

            gain = vcol[:, V_FG:V_FG + DK]

            def tokens_to_sbuf():
                for half in range(2):
                    last = v.tensor_tensor(xT[:, half * 4:half * 4 + 4, :], ps[:, 6 + half, :].rearrange("p (k q) -> p k q", q=P),
                                           gain[:, half * 4:half * 4 + 4].unsqueeze(2).broadcast_to([P, 4, P]), ALU.mult)
                last.then_inc(xT_ready, 1)

            n_tiles = dve.value_load(tab[0:1, TAB_T + E:TAB_T + E + 1], min_val=E, max_val=MAX_TILES)
            slots_of(0, st.settle)
            dve.wait_ge(slots_ready, 1)
            slots_to_sbuf(st.settle)
            st.settle(v.memset(ps[:, 4, :], 0.0))
            dve.sem_inc(yT_ready, 1)
            dve.sem_inc(hold_ready, 1)
            dve.wait_ge(x_turned, 1)
            tokens_to_sbuf()

            LOOP_STEPS = 9

            with dve.Fori(0, MAX_TILES) as i:
                with dve.If(i < n_tiles):
                    count = [0]

                    def steps(ins):
                        count[0] += 1
                        ins.then_inc(moe_step, 1)
                        dve.wait_ge(moe_step, i * LOOP_STEPS + count[0])

                    e = dve.value_load(tab[0:1, bass.ds(i + TAB_E, 1)], min_val=0, max_val=E - 1)
                    dve.wait_ge(hold_ready, i + 1)
                    v.tensor_copy(bias_t[:], biasT[:, bass.ds(e, 1), :].rearrange("p a b -> p (a b)"))
                    v.tensor_copy(gate_cur[:], gate_next[:])
                    steps(v.tensor_copy(idx_cur[:], idx_next[:]))
                    slots_of(i + 1, steps)
                    dve.wait_ge(slots_ready, i + 2)
                    dve.wait_ge(gathered, i * 16 + 16)
                    slots_to_sbuf(steps)
                    for a in range(2):
                        dve.wait_ge(used[4 * a + 3], i + 1)
                        if a:
                            dve.wait_ge(swiglu_done, i * 2 + 1)
                        v.tensor_tensor(u_in[:], ps[:, 2 * a + 1, :].rearrange("p (f q) -> p f q", q=P),
                                        bias_t[:, 8 + 4 * a:12 + 4 * a].unsqueeze(2).broadcast_to([P, 4, P]), ALU.add)
                        steps(v.tensor_tensor(g_in[:], ps[:, 2 * a, :].rearrange("p (f q) -> p f q", q=P),
                                              bias_t[:, 4 * a:4 * a + 4].unsqueeze(2).broadcast_to([P, 4, P]), ALU.add))
                        v.tensor_scalar(g_in[:], g_in[:], LIMIT, None, ALU.min).then_inc(gmin_ready, 1)
                        steps(v.tensor_scalar(u_in[:], u_in[:], LIMIT, -LIMIT, ALU.min, ALU.max))
                        dve.wait_ge(sig_ready, i * 2 + (a + 1))
                        steps(v.tensor_tensor(g_in[:], g_in[:], g_sig[:], ALU.mult))
                        v.scalar_tensor_tensor(out=act_T[:, 4 * a:4 * a + 4, :].rearrange("p f q -> p (f q)"),
                                               in0=u_in[:].rearrange("p f q -> p (f q)"), scalar=1.0,
                                               in1=g_in[:].rearrange("p f q -> p (f q)"), op0=ALU.add, op1=ALU.mult).then_inc(swiglu_done, 1)
                    dve.wait_ge(x_turned, i + 2)
                    tokens_to_sbuf()
                    dve.wait_ge(y_turned, i + 1)
                    dve.wait_ge(used[CHUNKS - 1], i + 1)
                    for half in range(2):
                        last = v.tensor_tensor(yT[:, half * 4:half * 4 + 4, :], ps[:, 4 + half, :].rearrange("p (d q) -> p d q", q=P),
                                               bias_t[:, 16 + half * 4:20 + half * 4].unsqueeze(2).broadcast_to([P, 4, P]), ALU.add)
                    last.then_inc(yT_ready, 1)
                    dve.wait_ge(yrow_ready, i + 1)
                    dve.wait_ge(scattered, i * 16 + 16)
                    v.tensor_copy(gate_hold[:], gate_cur[:])
                    v.tensor_copy(idx_hold[:], idx_cur[:]).then_inc(hold_ready, 1)
            assert count[0] == LOOP_STEPS


_INS = ["x", "positions", "norm_mix_g", "w_in", "q_latent_g", "w_uq", "kv_latent_g", "w_ukv", "q_head_g", "k_head_g",
        "conv_dw_w", "conv_dw_b", "conv_ln_g", "conv_ln_b", "attn_out_g", "conv_out_g", "w_out", "norm_ffn_g",
        "router_w", "router_b", "w_gate_up", "b_gate_up", "w_down", "b_down"]


def kernel(**inputs):
    import numpy as _np
    import concourse.bacc as _bacc
    from concourse import mybir as _mybir
    from concourse.bass_utils import run_bass_kernel_spmd as _run

    nc = _bacc.Bacc("TRN2", target_bir_lowering=False, num_devices=1)
    arrays, args = {}, {}
    for name in _INS:
        a = _np.ascontiguousarray(inputs[name])
        arrays[f"in_{name}"] = a
        args[name] = nc.dram_tensor(f"in_{name}", a.shape, _mybir.dt.from_np(a.dtype), kind="ExternalInput").ap()
    args["out"] = nc.dram_tensor("out_0", (1, T, D), _mybir.dt.float32, kind="ExternalOutput").ap()
    block_kernel(nc, args)
    r = _run(nc, [arrays], core_ids=[0])
    return r.results[0]["out_0"]
```

```python
from contextlib import ExitStack

import numpy as np
import concourse.bass as bass
from concourse import mybir

F32 = mybir.dt.float32
F32R = mybir.dt.float32r
I32 = mybir.dt.int32
U32 = mybir.dt.uint32
ALU = mybir.AluOpType
ACT = mybir.ActivationFunctionType
AX = mybir.AxisListType

P = 128
T = 512
TT = T // P
D = 1024
DK = D // P
Q_RANK, KV_RANK = 384, 128
QJ = Q_RANK // P
H, NOPE, ROPE, VD = 8, 64, 32, 64
HD = NOPE + ROPE
CONV = 512
CC = CONV // P
TAPS = 31
PAD = TAPS - 1
IN_W = Q_RANK + KV_RANK + ROPE + 2 * CONV
COL_ROPE = Q_RANK + KV_RANK
COL_A = COL_ROPE + ROPE
COL_G = COL_A + CONV
CHUNK = 64
E, TOPK, FF = 32, 4, 1024
EPS = 1e-6
SCALE = HD ** -0.5
ALPHA, LIMIT = 1.702, 7.0
MAX_TILES = E + (T * TOPK - 1) // P
TAB = 48
TAB_E, TAB_J, TAB_N, TAB_T = 0, TAB, 2 * TAB, 3 * TAB
NONE = 4096.0
SLOT_BYTES = 8192
RAW, SPLIT = 6, 4
GU0, DN1, GU1, DN0 = (0, 1, 2, 3), (4, 5), (6, 7, 8, 9), (10, 11)
CHUNKS = 12
POOL_LO = (0, 4)

V_MIX, V_QL, V_KL, V_DWB, V_LNG, V_LNB, V_AG, V_CG, V_FG, V_W = 0, 8, 11, 12, 16, 20, 24, 28, 32, 40
V_POS = V_W + TAPS * CC
V_ALL = V_POS + TT

TWO_PI = 2.0 * np.pi
PI2_A = 6.28125
PI2_B = float(np.round((TWO_PI - PI2_A) * 2.0 ** 19) / 2.0 ** 19)
PI2_C = TWO_PI - PI2_A - PI2_B
ROUND = 1.5 * 2.0 ** 23
PI_IN = float(np.float32(3.1415925))


def block_kernel(nc, A):
    with ExitStack() as ctx:
        base = (nc.sbuf_base + 63) // 64 * 64
        fence = ctx.enter_context(nc.sbuf_tensor("arena", [P, 53000], F32))
        del fence

        def at(name, offset, shape, dt=F32):
            return nc.alloc_sbuf_tensor_at(name, shape, dt, offset=base + offset)

        def sem(name):
            return ctx.enter_context(nc.semaphore(name))

        raw = [at(f"raw{r}", r * SLOT_BYTES, [P, 2, 1024]) for r in range(RAW)]
        w_hi = [at(f"w_hi{n}", (RAW + 2 * n) * SLOT_BYTES, [P, 2, 1024], F32R) for n in range(SPLIT)]
        w_lo = [at(f"w_lo{n}", (RAW + 2 * n + 1) * SLOT_BYTES, [P, 2, 1024], F32R) for n in range(SPLIT)]
        bias_raw = at("bias_raw", 49152, [2 * E, 3 * FF])
        ffn_gain = at("ffn_gain", 61440, [P, D])
        w_in = at("w_in", 0, [P, DK, IN_W])
        w_uq = at("w_uq", 50176, [P, QJ, H * HD])
        w_ukv = at("w_ukv", 59392, [P, 1024])
        w_out = at("w_out", 8 * SLOT_BYTES, [P, DK, D])
        qT = at("qT", 0, [HD, H, T])
        kT = at("kT", 16384, [HD, H, T])
        lnsq = at("lnsq", 32768, [P, CC, T])
        rowsq = at("rowsq", 40960, [P, 2, H * HD])
        o = 12 * SLOT_BYTES
        x = at("x", o, [P, TT, D]); o += 16384
        hT = at("hT", o, [P, DK, T])
        mixT = at("mixT", o, [P, DK, T])
        bias_hl = at("bias_hl", o, [2 * E, 3 * FF], F32R)
        yrow = at("yrow", o + 12288, [P, D]); o += 16384
        arena_moe = o
        ypad = at("ypad", o, [P, CC, PAD + T]); o += 8704
        cacc = at("cacc", o, [P, CC, T]); o += 8192
        xn = at("xn", o, [P, TT, D])
        latT = at("latT", o, [P, 4, T])
        attn_row = at("attn_row", o, [P, 2, T])
        latsq = at("latsq", o + 8192, [P, 4, T])
        h2T = at("h2T", o + 8192, [P, 2, DK, P]); o += 16384
        vrow = at("vrow", o, [P, TT, H * VD])
        hn = at("hn", o, [P, TT, D]); o += 8192
        sgl = at("sgl", o, [P, 2, T])
        rows = [at(f"rows{u}", a + 3072 * (u % 4 % 2 if u >= 4 else u), [P, H, HD]) for u, a in
                enumerate([o] * 4 + [arena_moe] * 2 + [arena_moe + 25088] * 2)]
        probs = at("probs", o, [P, 2, T])
        probsT = at("probsT", o + 4096, [P, 2, 4, P])
        vec_rows = at("vec_rows", o + 7168, [V_W, P])
        dw_rows = at("dw_rows", o + 7680, [TAPS * CC, P])
        pos_i = at("pos_i", o + 8192, [TT, P], I32)
        pos_f = at("pos_f", o + 8704, [TT, P])
        o += 12288
        m = arena_moe
        onehot = at("onehot", m, [P, TT, P]); m += 2048
        xg = at("xg", m, [P, D]); m += 4096
        x_hi = at("x_hi", m, [P, DK, P], F32R); m += 4096
        x_lo = at("x_lo", m, [P, DK, P], F32R); m += 4096
        g_in = at("g_in", m, [P, 512]); m += 2048
        u_in = at("u_in", m, [P, 512]); m += 2048
        g_sig = at("g_sig", m, [P, 512]); m += 2048
        act_row = at("act_row", m, [P, 512]); m += 2048
        a_hi = at("a_hi", m, [P, 8, P], F32R); m += 4096
        a_lo = at("a_lo", m, [P, 8, P], F32R); m += 4096
        sel = at("sel", m, [2 * E, P], F32R); m += 512
        assert m <= arena_moe + 8704 + 8192 + 16384

        def small(name, shape, dt=F32):
            nonlocal o
            n = int(np.prod(shape[1:])) * 4
            t = at(name, o, shape, dt)
            o += (n + 31) // 32 * 32
            return t

        ident = small("ident", [P, P])
        tri = small("tri", [P, P])
        ones = small("ones", [P, P])
        inv_c = small("inv_c", [P, P])
        iota_s = small("iota_s", [P, T])
        inv_freq = small("inv_freq", [P, ROPE // 2])
        tokv = small("tokv", [P, TT, 3])
        slot_row = small("slot_row", [P, 1])
        eidx = small("eidx", [E, 1])
        eps = small("eps", [P, 1])
        vcol = small("vcol", [P, V_ALL])
        pick = small("pick", [2 * E, E])
        qk_gain = small("qk_gain", [P, 2, HD])
        router = small("router", [P, DK, E])
        router_bias = small("router_bias", [P, E])
        ssx = small("ssx", [P, TT]); stdx = small("stdx", [P, TT]); rsx = small("rsx", [P, TT])
        ang = small("ang", [P, TT, 16]); turns = small("turns", [P, 2, TT, 16])
        red = small("red", [P, 2, TT, 16])
        cosd = small("cosd", [P, TT, 2, 16]); sin_ = small("sin_", [P, TT, 16]); nsin = small("nsin", [P, TT, 16])
        krope = small("krope", [P, TT, ROPE])
        lat_std = small("lat_std", [P, 8]); lat_rs = small("lat_rs", [P, 8])
        ln_std = small("ln_std", [P, T])
        css = small("css", [P, TT]); c_rs = small("c_rs", [P, TT])
        hss = small("hss", [P, 8, H]); hstd = small("hstd", [P, 8, H]); hrs = small("hrs", [P, 8, H])
        rtmp = small("rtmp", [P, 2, H, ROPE])
        mx = small("mx", [P, 32]); nmx = small("nmx", [P, 32]); den = small("den", [P, TT, H]); rden = small("rden", [P, TT, H])
        ass_ = small("ass", [P, TT]); astd = small("astd", [P, TT]); a_rs = small("a_rs", [P, TT])
        ss1 = small("ss1", [P, TT]); std1 = small("std1", [P, TT]); rs1 = small("rs1", [P, TT])
        logits = small("logits", [P, TT, E])
        top_v = small("top_v", [P, TT, 8]); top_i = small("top_i", [P, TT, 8], U32); top_f = small("top_f", [P, TT, 4])
        hot = at("hot", arena_moe, [P, 16, E])
        hotg = at("hotg", arena_moe + 2048, [P, 16, E])
        tg = small("tg", [P, TT, 4]); tgs = small("tgs", [P, TT]); tgr = small("tgr", [P, TT])
        mask = small("mask", [P, TT, E]); gate = small("gate", [P, TT, E]); posm = small("posm", [P, TT, E])
        cnt = small("cnt", [E, 4]); member = small("member", [E, TAB]); memj = small("memj", [E, TAB]); memn = small("memn", [E, TAB])
        tab = small("tab", [1, 4 * TAB], I32)
        slot_f = small("slot_f", [P, 2])
        gate_next = small("gate_next", [P, 1]); idx_next = small("idx_next", [P, 1], I32)
        gate_cur = small("gate_cur", [P, 1]); idx_cur = small("idx_cur", [P, 1], I32)
        gate_hold = small("gate_hold", [P, 1]); idx_hold = small("idx_hold", [P, 1], I32)
        assert o <= 53000 * 4, o

        ps = ctx.enter_context(nc.psum_tensor("ps", [P, 8, 512], F32))
        h_rows = nc.dram_tensor("h_rows", [T + P, D], F32, kind="Internal").ap()
        acc = nc.dram_tensor("acc", [T + P, D], F32, kind="Internal").ap()

        x_landed = [sem(f"x_landed{t}") for t in range(TT)]
        w_in_landed = [sem(f"w_in_landed{k}") for k in range(DK)]
        small_landed, router_landed, bias_landed = sem("small_landed"), sem("router_landed"), sem("bias_landed")
        wqkv_landed, w_out_landed, gain_landed = sem("wqkv_landed"), sem("w_out_landed"), sem("gain_landed")
        consts, pool_step, act_step, dve_step = sem("consts"), sem("pool_step"), sem("act_step"), sem("dve_step")
        posf_ready, cols_turned, cols_ready = sem("posf_ready"), sem("cols_turned"), sem("cols_ready")
        xstd_ready, xn_ready, x_turned0 = sem("xstd_ready"), sem("xn_ready"), sem("x_turned0")
        hT_dve, hT_act = sem("hT_dve"), sem("hT_act")
        pair_ready, sg_ready, glu_done = sem("pair_ready"), sem("sg_ready"), sem("glu_done")
        ang_ready, trig_ready = sem("ang_ready"), sem("trig_ready")
        lat_ready, lat_sq, lat_done = sem("lat_ready"), sem("lat_sq"), sem("lat_done")
        krope_ready, krope_copied, lat_ss, lat_std_ready, lat_rs_ready = (
            sem("krope_ready"), sem("krope_copied"), sem("lat_ss"), sem("lat_std_ready"), sem("lat_rs_ready"))
        bias_hi_ready, bias_ready = sem("bias_hi_ready"), sem("bias_ready")
        rows_ready, rows_out, rowsq_ready, hss_ready, hstd_ready, headnorm = (
            sem("rows_ready"), sem("rows_out"), sem("rowsq_ready"), sem("hss_ready"), sem("hstd_ready"), sem("headnorm"))
        gained, roped, rows_turned, rowsT_out = sem("gained"), sem("roped"), sem("rows_turned"), sem("rowsT_out")
        conv_done, ln_mean, ln_xc, ln_sq, ln_var, ln_stdr = (
            sem("conv_done"), sem("ln_mean"), sem("ln_xc"), sem("ln_sq"), sem("ln_var"), sem("ln_stdr"))
        ln_norm, ln_sig, ln_silu, conv_sq, conv_ss, conv_std, conv_mix, conv_out, conv_added = (
            sem("ln_norm"), sem("ln_sig"), sem("ln_silu"), sem("conv_sq"), sem("conv_ss"), sem("conv_std"), sem("conv_mix"), sem("conv_out"), sem("conv_added"))
        s_ready, max_ready, exp_ready, pT_ready, pT_out, pv_done = (
            sem("s_ready"), sem("max_ready"), sem("exp_ready"), sem("pT_ready"), sem("pT_out"), sem("pv_done"))
        o_normed, a_ss_ready, o_turned, attn_mix, a_std_ready = (
            sem("o_normed"), sem("a_ss_ready"), sem("o_turned"), sem("attn_mix"), sem("a_std_ready"))
        out_ready, x1_ready, std1_ready, hn_ready, hn_turned, h2_act, h2_dve, log_ready, log_out = (
            sem("out_ready"), sem("x1_ready"), sem("std1_ready"), sem("hn_ready"), sem("hn_turned"),
            sem("h2_act"), sem("h2_dve"), sem("log_ready"), sem("log_out"))
        stored = sem("stored")
        topd_ready, texp_ready, mask_ready, pos_ready, nt_ready, start_ready, mem_ready, fields_ready, tab_ready = (
            sem("topd_ready"), sem("texp_ready"), sem("mask_ready"), sem("pos_ready"), sem("nt_ready"),
            sem("start_ready"), sem("mem_ready"), sem("fields_ready"), sem("tab_ready"))
        landed = [sem(f"landed{r}") for r in range(RAW)]
        raw_free = [sem(f"raw_free{r}") for r in range(RAW)]
        hi_done, split_free = sem("hi_done"), sem("split_free")
        hot_ready, slots_ready, slots_out, gathered = sem("hot_ready"), sem("slots_ready"), sem("slots_out"), sem("gathered")
        x_turned, x_hi_ready, x_ready, sel_ready, sel_used = (
            sem("x_turned"), sem("x_hi_ready"), sem("x_ready"), sem("sel_ready"), sem("sel_used"))
        gmin_ready, sig_ready, act_ready = sem("gmin_ready"), sem("sig_ready"), sem("act_ready")
        act_turned, a_hi_ready, a_ready = sem("act_turned"), sem("a_hi_ready"), sem("a_ready")
        yrow_ready, hold_ready, scattered = sem("yrow_ready"), sem("hold_ready"), sem("scattered")
        pool_go, moe_step, final = sem("pool_go"), sem("moe_step"), sem("final")

        N_SMALL = 14
        block = ctx.enter_context(nc.Block())

        unit_bank = (6, 0, 2, 0, 6, 2, 6, 2)

        def turn_bank(u):
            return 0 if u % 2 else 4

        class Steps:

            def __init__(self, eng, s):
                self.eng, self.s, self.n = eng, s, 0

            def mark(self, ins):
                self.n += 1
                ins.then_inc(self.s, 1)
                return self.n

            def settle(self, ins):
                self.eng.wait_ge(self.s, self.mark(ins))

        def chunk_ready(i, q):
            return i * 2 + (q // RAW + 2)

        def multiplied(i, q):
            return i * CHUNKS + (q + 1 + SPLIT)

        @block.sync
        def _(sp):
            for t in range(TT):
                sp.dma_start(x[:, t, :], A["x"][0, t * P:(t + 1) * P, :]).then_inc(x_landed[t], 16)
            sp.wait_ge(small_landed, 16 * N_SMALL)
            for k in range(DK):
                sp.dma_start(w_in[:, k, :], A["w_in"][0, k * P:(k + 1) * P, :]).then_inc(w_in_landed[k], 16)
            sp.dma_start(w_uq[:], A["w_uq"][0].rearrange("(j p) n -> p j n", p=P)).then_inc(wqkv_landed, 16)
            sp.dma_start(w_ukv[:], A["w_ukv"][0]).then_inc(wqkv_landed, 16)
            sp.dma_start(w_out[:], A["w_out"][0].rearrange("(k p) n -> p k n", p=P)).then_inc(w_out_landed, 16)

            def load_chunk(e, q, r):
                for kk in range(2):
                    if q in GU0 or q in GU1:
                        a, k = (0, q * 2 + kk) if q in GU0 else (1, (q - GU1[0]) * 2 + kk)
                        sp.dma_start(raw[r][:, kk].rearrange("p (g f) -> p g f", g=2),
                                     A["w_gate_up"][0, e, k * P:(k + 1) * P, :].rearrange(
                            "p (g a f) -> a p g f", g=2, a=2)[a]).then_inc(landed[r], 16)
                    else:
                        k = (4 + (q - DN1[0]) * 2 if q in DN1 else (q - DN0[0]) * 2) + kk
                        sp.dma_start(raw[r][:, kk], A["w_down"][0, e, k * P:(k + 1) * P, :]).then_inc(landed[r], 16)

            sp.wait_ge(s_ready, TT * H)
            sp.wait_ge(ln_silu, 1)
            sp.wait_ge(conv_ss, 1)
            sp.dma_start(ffn_gain[:], A["norm_ffn_g"].broadcast_to([P, D])).then_inc(gain_landed, 16)
            for q in range(RAW):
                load_chunk(0, q, q)
            for n in range(2):
                sp.dma_start(bias_raw[n * E:(n + 1) * E, 0:2 * FF], A["b_gate_up"][0]).then_inc(bias_landed, 16)
                sp.dma_start(bias_raw[n * E:(n + 1) * E, 2 * FF:], A["b_down"][0]).then_inc(bias_landed, 16)
            for t in range(TT):
                sp.wait_ge(x1_ready, t + 1)
                sp.dma_start(acc[t * P:(t + 1) * P, :], x[:, t, :]).then_inc(stored, 16)
                if t == 0:
                    sp.dma_start(acc[T:T + P, :], x[:, t, :]).then_inc(stored, 16)
                sp.wait_ge(hn_ready, t + 1)
                sp.dma_start(h_rows[t * P:(t + 1) * P, :], hn[:, t, :]).then_inc(stored, 16)
                if t == 0:
                    sp.dma_start(h_rows[T:T + P, :], hn[:, t, :]).then_inc(stored, 16)
            for q in range(RAW, CHUNKS):
                sp.wait_ge(raw_free[q - RAW], 2)
                load_chunk(0, q, q - RAW)
            sp.wait_ge(tab_ready, 1)
            tiles = sp.value_load(tab[0:1, TAB_T + E:TAB_T + E + 1], min_val=E, max_val=MAX_TILES)
            with sp.Fori(1, MAX_TILES) as i:
                with sp.If(i < tiles):
                    e = sp.value_load(tab[0:1, bass.ds(i + TAB_E, 1)], min_val=0, max_val=E - 1)
                    e_last = sp.value_load(tab[0:1, bass.ds(i + (TAB_E - 1), 1)], min_val=0, max_val=E - 1)
                    for q in range(CHUNKS):
                        sp.wait_ge(raw_free[q % RAW], i * 2 + (q // RAW + 1))
                        load_chunk(e_last if q in DN1 else e, q, q % RAW)
            for r, q in enumerate(DN1):
                sp.wait_ge(raw_free[r], tiles * 2 + 1)
                load_chunk(E - 1, q, r)
            sp.wait_ge(scattered, tiles * 16 + 16)
            sp.dma_start(A["out"][0], acc[0:T, :]).then_inc(final, 16)
            sp.wait_ge(final, 16)

        @block.gpsimd
        def _(pool):
            st = Steps(pool, pool_step)
            g = nc.gpsimd
            g.memset(ident[:], 0.0).then_inc(pool_step, 1)
            g.memset(tri[:], 1.0).then_inc(pool_step, 1)
            g.memset(ones[:], 1.0).then_inc(consts, 1)
            g.memset(inv_c[:], 1.0 / CONV).then_inc(consts, 1)
            st.n = 2
            pool.wait_ge(pool_step, 2)
            g.affine_select(out=ident[:], in_=ident[:], compare_op=ALU.not_equal, fill=1.0, base=0,
                            pattern=[[-1, P]], channel_multiplier=1).then_inc(consts, 1)
            g.affine_select(out=tri[:], in_=tri[:], compare_op=ALU.is_gt, fill=0.0, base=0,
                            pattern=[[1, P]], channel_multiplier=-1).then_inc(consts, 1)
            g.memset(eps[:], EPS).then_inc(consts, 1)
            freq = np.float32(1) / np.float32(10000) ** (np.arange(0, ROPE, 2, dtype=np.float32) / np.float32(ROPE))
            for n in range(ROPE // 2):
                g.memset(inv_freq[:, n:n + 1], float(freq[n])).then_inc(consts, 1)
            g.memset(ypad[:, :, 0:PAD], 0.0).then_inc(consts, 1)
            g.iota(iota_s[:], [[1, T]], base=0, channel_multiplier=0,
                   allow_small_or_imprecise_dtypes=True).then_inc(consts, 1)
            g.iota(slot_row[:], [[0, 1]], base=T, channel_multiplier=1,
                   allow_small_or_imprecise_dtypes=True).then_inc(consts, 1)
            g.iota(eidx[:], [[0, 1]], base=0, channel_multiplier=1,
                   allow_small_or_imprecise_dtypes=True).then_inc(consts, 1)
            g.iota(tokv[:, :, 0], [[P, TT]], base=0, channel_multiplier=1,
                   allow_small_or_imprecise_dtypes=True).then_inc(consts, 1)
            g.memset(tokv[:, :, 1], 1.0).then_inc(consts, 1)
            g.iota(idx_hold[:], [[0, 1]], base=T, channel_multiplier=1).then_inc(consts, 1)
            g.memset(gate_hold[:], 0.0).then_inc(consts, 1)
            pool.wait_ge(small_landed, 16 * N_SMALL)
            for u in range(2 * TT):
                pool.wait_ge(headnorm, u + 1)
                r = rows[u]
                g.tensor_tensor(r[:], r[:], qk_gain[:, u % 2, :].unsqueeze(1).broadcast_to([P, H, HD]),
                                ALU.mult).then_inc(gained, 1)
            pool.wait_ge(bias_hi_ready, 1)
            g.tensor_tensor(bias_hl[E:2 * E], bias_raw[E:2 * E], bias_hl[E:2 * E].bitcast(F32), ALU.subtract).then_inc(bias_ready, 1)
            def first_low_part(q):
                pool.wait_ge(hi_done, q + 1)
                g.tensor_tensor(w_lo[q][:], raw[q][:], w_hi[q][:].bitcast(F32), ALU.subtract).then_inc(raw_free[q], 1)

            for q in (0, 1):
                first_low_part(q)
            pool.wait_ge(tab_ready, 1)
            n_tiles = pool.value_load(tab[0:1, TAB_T + E:TAB_T + E + 1], min_val=E, max_val=MAX_TILES)
            pool.wait_ge(stored, 16 * 2 * (TT + 1))

            def gather(rows):
                pool.indirect_dma_start(out=xg[0:rows], out_offset=None, in_=h_rows,
                                        in_offset=bass.IndirectOffsetOnAxis(ap=idx_next[0:rows, 0:1], axis=0),
                                        bounds_check=T + P - 1).then_inc(gathered, 16)

            def scatter(rows):
                pool.indirect_dma_start(out=acc, out_offset=bass.IndirectOffsetOnAxis(ap=idx_hold[0:rows, 0:1], axis=0),
                                        in_=yrow[0:rows], in_offset=None, bounds_check=T + P - 1,
                                        compute_op=ALU.add).then_inc(scattered, 16)

            def move(op, n):
                with pool.If(n < 65):
                    op(64)
                with pool.Else():
                    with pool.If(n < 97):
                        op(96)
                    with pool.Else():
                        op(P)

            def low_part(i, q):
                pool.wait_ge(hi_done, i * CHUNKS + (q + 1))
                pool.sem_inc(pool_go, 1)
                g.tensor_tensor(w_lo[q % SPLIT][:], raw[q % RAW][:], w_hi[q % SPLIT][:].bitcast(F32),
                                ALU.subtract).then_inc(raw_free[q % RAW], 1)

            pool.wait_ge(slots_out, 1)
            gather(P)
            for q in (2, 3):
                first_low_part(q)
            with pool.Fori(0, MAX_TILES) as i:
                with pool.If(i < n_tiles):
                    n_next = pool.value_load(tab[0:1, bass.ds(i + (TAB_N + 1), 1)], min_val=0, max_val=T)
                    n_last = pool.value_load(tab[0:1, bass.ds(i + (TAB_N - 1), 1)], min_val=0, max_val=T)
                    with pool.If(i > 0):
                        low_part(i, POOL_LO[0])
                    low_part(i, POOL_LO[1])
                    pool.wait_ge(slots_out, i + 2)
                    pool.sem_inc(pool_go, 1)
                    pool.wait_ge(x_turned, i + 1)
                    pool.sem_inc(pool_go, 1)
                    move(gather, n_next)
                    pool.wait_ge(yrow_ready, i + 1)
                    pool.sem_inc(pool_go, 1)
                    move(scatter, n_last)
            pool.wait_ge(yrow_ready, n_tiles + 1)
            pool.sem_inc(pool_go, 1)
            scatter(P)

        @block.tensor
        def _(pe):
            mm, tr = nc.tensor.matmul, nc.tensor.transpose
            for r in range(RAW):
                pe.sem_inc(raw_free[r], 1)
            pe.wait_ge(consts, 13 + ROPE // 2)
            pe.wait_ge(small_landed, 16 * N_SMALL)
            tr(ps[:, 7, 0:V_W], vec_rows[:], ident[0:V_W, 0:V_W])
            tr(ps[:, 7, V_W:V_POS], dw_rows[:], ident[0:TAPS * CC, 0:TAPS * CC])
            pe.wait_ge(posf_ready, 1)
            tr(ps[:, 7, V_POS:V_ALL], pos_f[:], ident[0:TT, 0:TT]).then_inc(cols_turned, 1)
            pe.wait_ge(cols_ready, 1)
            for t in range(TT):
                pe.wait_ge(xn_ready, t + 1)
                for k in range(DK):
                    last = tr(ps[:, k, t * P:(t + 1) * P], xn[:, t, k * P:(k + 1) * P], ident[:])
            last.then_inc(x_turned0, 1)

            pe.wait_ge(hT_dve, 4)
            pe.wait_ge(hT_act, 4)
            conv_cols = [c for n in range(CC) for c in (COL_A + n * P, COL_G + n * P)]
            for k in range(DK):
                pe.wait_ge(w_in_landed[k], 16)
                for b in range(4):
                    last = mm(ps[:, b, :], w_in[:, k, conv_cols[b]:conv_cols[b] + P], hT[:, k, :],
                              start=(k == 0), stop=(k == DK - 1))
            last.then_inc(pair_ready, 2)
            for b in range(4, 8):
                for k in range(DK):
                    last = mm(ps[:, b, :], w_in[:, k, conv_cols[b]:conv_cols[b] + P], hT[:, k, :],
                              start=(k == 0), stop=(k == DK - 1))
                if b % 2:
                    last.then_inc(pair_ready, 1)
            pe.wait_ge(glu_done, 2)
            for j in range(4):
                for k in range(DK):
                    last = mm(ps[:, j, :], w_in[:, k, j * P:(j + 1) * P], hT[:, k, :],
                              start=(k == 0), stop=(k == DK - 1))
                last.then_inc(lat_ready, 1)
            pe.wait_ge(glu_done, 3)
            for t in range(TT):
                for k in range(DK):
                    last = mm(ps[:, 4, t * ROPE:(t + 1) * ROPE], hT[:, k, t * P:(t + 1) * P],
                              w_in[:, k, COL_ROPE:COL_A], start=(k == 0), stop=(k == DK - 1))
            last.then_inc(krope_ready, 1)
            pe.wait_ge(lat_sq, 4)
            for t in range(TT):
                for j in range(QJ):
                    mm(ps[:, 5, t:t + 1], latsq[:, j, t * P:(t + 1) * P], ones[:, 0:1], start=(j == 0), stop=(j == QJ - 1))
                last = mm(ps[:, 5, 4 + t:5 + t], latsq[:, 3, t * P:(t + 1) * P], ones[:, 0:1], start=True, stop=True)
            last.then_inc(lat_ss, 1)
            pe.wait_ge(glu_done, 4)

            def up_queries(t):
                for half in range(2):
                    for j in range(QJ):
                        last = mm(ps[:, unit_bank[2 * t] + half, 0:Q_RANK], latT[:, j, t * P:(t + 1) * P],
                                  w_uq[:, j, half * Q_RANK:(half + 1) * Q_RANK], start=(j == 0), stop=(j == QJ - 1))
                last.then_inc(rows_ready, 1)

            def up_keys(t):
                for half in range(2):
                    last = mm(ps[:, unit_bank[2 * t + 1] + half, :], latT[:, 3, t * P:(t + 1) * P],
                              w_ukv[:, half * 512:(half + 1) * 512], start=True, stop=True)
                last.then_inc(rows_ready, 1)

            pe.wait_ge(wqkv_landed, 32)
            pe.wait_ge(lat_done, 4)
            up_queries(0)
            up_keys(0)
            pe.wait_ge(krope_copied, 1)
            pe.wait_ge(lat_std_ready, 1)
            up_queries(1)
            pe.wait_ge(rows_out, 2)
            up_keys(1)
            pe.wait_ge(conv_done, 1)
            for c in range(CC):
                last = mm(ps[:, 4, :], inv_c[:], cacc[:, c, :], start=(c == 0), stop=(c == CC - 1))
            last.then_inc(ln_mean, 1)
            up_queries(2)
            pe.wait_ge(ln_sq, 1)
            for c in range(CC):
                last = mm(ps[:, 5, :], inv_c[:], lnsq[:, c, :], start=(c == 0), stop=(c == CC - 1))
            last.then_inc(ln_var, 1)
            pe.wait_ge(rows_out, 3)
            up_keys(2)
            pe.wait_ge(rows_out, 5)
            up_queries(3)
            pe.wait_ge(rows_out, 6)
            up_keys(3)
            pe.wait_ge(conv_sq, 1)
            for t in range(TT):
                for c in range(CC):
                    last = mm(ps[:, 5, t:t + 1], lnsq[:, c, t * P:(t + 1) * P], ones[:, 0:1], start=(c == 0), stop=(c == CC - 1))
            last.then_inc(conv_ss, 1)

            def conv_part(t, n):
                half, k = n // 4, n % 4
                last = mm(ps[:, (2 if t == 0 else 6) + half, :], mixT[:, 4 + k, t * P:(t + 1) * P],
                          w_out[:, 4 + k, half * 512:(half + 1) * 512], start=(k == 0), stop=(k == 3))
                if n == 7:
                    last.then_inc(conv_out, 1)

            pe.wait_ge(w_out_landed, 16)
            for u in range(2 * TT):
                pe.wait_ge(roped, u + 1)
                if u == 0:
                    pe.wait_ge(conv_std, 1)
                if u >= 2:
                    pe.wait_ge(rowsT_out, u - 1)
                for h in range(H):
                    last = tr(ps[0:HD, turn_bank(u) + h // 4, (h % 4) * P:(h % 4 + 1) * P], rows[u][:, h, :], ident[:])
                last.then_inc(rows_turned, 1)
                if u == 0:
                    pe.wait_ge(conv_mix, 4)
                    pe.wait_ge(rows_out, 8)
                conv_part(u // 4, u % 4 * 2)
                conv_part(u // 4, u % 4 * 2 + 1)

            pe.wait_ge(rowsT_out, 8)

            def scores(s):
                qb, h = s // H, s % H
                if s >= 2:
                    pe.wait_ge(exp_ready, s - 1)
                mm(ps[:, s % 2, 0:(qb + 1) * P], qT[:, h, qb * P:(qb + 1) * P], kT[:, h, 0:(qb + 1) * P],
                   start=True, stop=True).then_inc(s_ready, 1)

            def turn_probs(s):
                qb = s // H
                pe.wait_ge(exp_ready, s + 1)
                if s >= 2:
                    pe.wait_ge(pT_out, s - 1)
                for n in range(qb + 1):
                    last = tr(ps[:, 2 + s % 2, n * P:(n + 1) * P], probs[:, s % 2, n * P:(n + 1) * P], ident[:])
                last.then_inc(pT_ready, 1)

            def weigh_values(s):
                qb, h = s // H, s % H
                pe.wait_ge(pT_out, s + 1)
                if h == 0 and qb >= 2:
                    pe.wait_ge(attn_mix, qb - 1)
                for n in range(qb + 1):
                    last = mm(ps[:, 4 + qb % 2, h * VD:(h + 1) * VD], probsT[:, s % 2, n, :],
                              vrow[:, n, h * VD:(h + 1) * VD], start=(n == 0), stop=(n == qb))
                last.then_inc(pv_done, 1)

            def turn_attention(qb):
                pe.wait_ge(o_normed, qb + 1)
                for n in range(4):
                    last = tr(ps[:, 4 + qb % 2, n * P:(n + 1) * P], attn_row[:, qb % 2, n * P:(n + 1) * P], ident[:])
                last.then_inc(o_turned, 1)

            for s in range(TT * H + 6):
                if s < TT * H:
                    scores(s)
                if s % 9 < 8 and s < 17:
                    if s % 9 == 0:
                        pe.wait_ge(conv_added, s // 9 + 2)
                    conv_part(s // 9 + 2, s % 9)
                if 1 <= s <= TT * H:
                    turn_probs(s - 1)
                if 2 <= s <= TT * H + 1:
                    weigh_values(s - 2)
                if s >= 13 and (s - 13) % H == 0:
                    turn_attention((s - 13) // H)

            def project_out(t):
                b = 4 * (t % 2)
                for half in range(2):
                    for k in range(4):
                        last = mm(ps[:, b + half, :], mixT[:, k, t * P:(t + 1) * P],
                                  w_out[:, k, half * 512:(half + 1) * 512], start=(k == 0), stop=(k == 3))
                last.then_inc(out_ready, 1)

            def route(t):
                b = 4 * (t % 2)
                pe.wait_ge(hn_ready, t + 1)
                for k in range(DK):
                    last = tr(ps[:, b + k // 4, (k % 4) * P:(k % 4 + 1) * P], hn[:, t, k * P:(k + 1) * P], ident[:])
                last.then_inc(hn_turned, 1)
                pe.wait_ge(h2_act, t + 1)
                pe.wait_ge(h2_dve, t + 1)
                for k in range(DK):
                    last = mm(ps[:, b + 2, 0:E], h2T[:, t % 2, k, :], router[:, k, :], start=(k == 0), stop=(k == DK - 1))
                last.then_inc(log_ready, 1)

            pe.wait_ge(attn_mix, TT)
            pe.wait_ge(conv_added, TT)
            pe.wait_ge(router_landed, 16)
            project_out(0)
            project_out(1)
            route(0)
            pe.wait_ge(log_out, 1)
            project_out(2)
            route(1)
            pe.wait_ge(log_out, 2)
            project_out(3)
            route(2)
            route(3)

            pe.wait_ge(mask_ready, 1)
            for t in range(TT):
                for n in range(t):
                    mm(ps[:, 0, t * E:(t + 1) * E], ones[:], mask[:, n, :], start=(n == 0), stop=False)
                mm(ps[:, 0, t * E:(t + 1) * E], tri[:], mask[:, t, :], start=(t == 0), stop=True)
            for t in range(TT):
                last = mm(ps[0:E, 1, 0:1], mask[:, t, :], ones[:, 0:1], start=(t == 0), stop=(t == TT - 1))
            last.then_inc(pos_ready, 1)
            pe.wait_ge(nt_ready, 1)
            mm(ps[0:E, 1, 4:5], tri[0:E, 0:E], cnt[:, 1:2], start=True, stop=True)
            mm(ps[0:1, 1, 8:8 + E + 1], cnt[:, 1:2], tri[0:E, 0:E + 1], start=True, stop=True).then_inc(start_ready, 1)
            pe.wait_ge(mem_ready, 1)
            mm(ps[0:1, 2, TAB_E:TAB_E + TAB], eidx[:], member[:], start=True, stop=True)
            mm(ps[0:1, 2, TAB_J:TAB_J + TAB], ones[0:E, 0:1], memj[:], start=True, stop=True)
            mm(ps[0:1, 2, TAB_N:TAB_N + TAB], ones[0:E, 0:1], memn[:], start=True, stop=True).then_inc(fields_ready, 1)

            def fill_slots():
                for t in range(TT):
                    last = mm(ps[:, 6, 0:3], onehot[:, t, :], tokv[:, t, :], start=(t == 0), stop=(t == TT - 1))
                last.then_inc(slots_ready, 1)

            def turn_x():
                for k in range(DK):
                    last = tr(ps[:, 6 + k // 4, (k % 4) * P:(k % 4 + 1) * P], xg[:, k * P:(k + 1) * P], ident[:])
                last.then_inc(x_turned, 1)

            def turn_act(half):
                for k in range(4):
                    last = tr(ps[:, 7 - half, k * P:(k + 1) * P], act_row[:, k * P:(k + 1) * P], ident[:])
                last.then_inc(act_turned, 1)

            def bias(bank, col):
                return mm(ps[:, bank, :], sel[:], bias_hl[:, col:col + 512], start=True, stop=False,
                          skip_group_check=True)

            def chunk(i, q, slots, k0, banks, rows_hi, rows_lo, last_one):
                r, n = slots
                pe.wait_ge(raw_free[r], chunk_ready(i, q))
                for kk in range(2):
                    k = k0 + kk
                    for h, bank in enumerate(banks):
                        hi = w_hi[n][:, kk, h * 512:(h + 1) * 512]
                        mm(ps[:, bank, :], rows_hi[:, k, :], hi, start=False, stop=False, skip_group_check=True)
                        mm(ps[:, bank, :], rows_hi[:, k, :], w_lo[n][:, kk, h * 512:(h + 1) * 512], start=False,
                           stop=False, skip_group_check=True)
                        last = mm(ps[:, bank, :], rows_lo[:, k, :], hi, start=False, stop=last_one and kk == 1,
                                  skip_group_check=True)
                last.then_inc(split_free, 1)

            def gate_up(i, a, qs):
                for q in qs:
                    chunk(i, q, (q % RAW, q % SPLIT), (q - (GU1 if a else GU0)[0]) * 2, (2 * a, 2 * a + 1), x_hi, x_lo,
                          q in (GU0[-1], GU1[-1]))

            pe.wait_ge(tab_ready, 1)
            pe.wait_ge(bias_ready, 1)
            n_tiles = pe.value_load(tab[0:1, TAB_T + E:TAB_T + E + 1], min_val=E, max_val=MAX_TILES)
            pe.sem_inc(split_free, SPLIT)
            pe.sem_inc(sel_used, 1)
            pe.wait_ge(hot_ready, 1)
            fill_slots()
            pe.wait_ge(gathered, 16)
            turn_x()
            with pe.Fori(0, MAX_TILES) as i:
                with pe.If(i < n_tiles):
                    pe.wait_ge(sel_ready, i + 1)
                    pe.wait_ge(x_ready, i + 1)
                    for gu in range(2):
                        bias(gu, gu * FF)
                    gate_up(i, 0, GU0[:2])
                    pe.wait_ge(act_ready, i * 2 + 1)
                    turn_act(1)
                    gate_up(i, 0, GU0[2:])
                    pe.wait_ge(a_hi_ready, i * 2 + 1)
                    pe.wait_ge(a_ready, i * 2 + 1)
                    pe.wait_ge(hot_ready, i + 2)
                    fill_slots()
                    for q in DN1:
                        chunk(i, q, (q % RAW, q % SPLIT), 4 + (q - DN1[0]) * 2, (4, 5), a_hi, a_lo, q == DN1[-1])
                    for gu in range(2):
                        bias(2 + gu, gu * FF + 512)
                    gate_up(i, 1, GU1[:2])
                    pe.wait_ge(act_ready, i * 2 + 2)
                    turn_act(0)
                    gate_up(i, 1, GU1[2:])
                    pe.wait_ge(a_hi_ready, i * 2 + 2)
                    pe.wait_ge(a_ready, i * 2 + 2)
                    pe.wait_ge(slots_out, i + 2)
                    pe.wait_ge(gathered, i * 16 + 32)
                    turn_x()
                    pe.wait_ge(yrow_ready, i + 1)
                    bias(4, 2 * FF)
                    bias(5, 2 * FF + 512).then_inc(sel_used, 1)
                    for q in DN0:
                        chunk(i, q, (q % RAW, q % SPLIT), (q - DN0[0]) * 2, (4, 5), a_hi, a_lo, False)
            pe.wait_ge(act_ready, n_tiles * 2 + 1)
            turn_act(1)
            pe.wait_ge(a_hi_ready, n_tiles * 2 + 1)
            pe.wait_ge(a_ready, n_tiles * 2 + 1)
            for r, q in enumerate(DN1):
                chunk(n_tiles, r, (r, r), 4 + 2 * r, (4, 5), a_hi, a_lo, r == 1)

        @block.scalar
        def _(act):
            st = Steps(act, act_step)
            f = nc.scalar.activation

            def load(dst, src, s=small_landed):
                act.dma_start(dst, src).then_inc(s, 16)

            for col, name in ((V_MIX, "norm_mix_g"), (V_QL, "q_latent_g"), (V_KL, "kv_latent_g"), (V_DWB, "conv_dw_b"),
                              (V_LNG, "conv_ln_g"), (V_LNB, "conv_ln_b"), (V_AG, "attn_out_g"), (V_CG, "conv_out_g"),
                              (V_FG, "norm_ffn_g")):
                v = A[name][0].rearrange("(r c) -> r c", c=P)
                load(vec_rows[col:col + v.shape[0], :], v)
            load(dw_rows[:], A["conv_dw_w"][0].rearrange("j (c p) -> (j c) p", p=P))
            load(pos_i[:], A["positions"][0].rearrange("(t p) -> t p", p=P))
            load(qk_gain[:, 0, :], A["q_head_g"].broadcast_to([P, HD]))
            load(qk_gain[:, 1, :], A["k_head_g"].broadcast_to([P, HD]))
            load(router_bias[:], A["router_b"].broadcast_to([P, E]))
            load(router[:], A["router_w"][0].rearrange("(k p) e -> p k e", p=P), router_landed)

            act.wait_ge(consts, 13 + ROPE // 2)
            for t in range(TT):
                act.wait_ge(x_landed[t], 16)
                st.settle(f(xn[:, t, :], x[:, t, :], ACT.Square, accum_out=ssx[:, t:t + 1]))
                f(stdx[:, t:t + 1], ssx[:, t:t + 1], ACT.Sqrt, bias=eps[:, 0:1], scale=1.0 / D).then_inc(xstd_ready, 1)
            act.wait_ge(cols_ready, 1)
            act.wait_ge(x_turned0, 1)
            for k in range(1, DK, 2):
                f(hT[:, k, :], ps[:, k, :], ACT.Copy, scale=vcol[:, V_MIX + k:V_MIX + k + 1]).then_inc(hT_act, 1)
            act.wait_ge(ang_ready, 1)
            f(sin_[:], red[:, 0], ACT.Sin).then_inc(trig_ready, 1)
            f(cosd[:, :, 0, :], red[:, 1], ACT.Sin).then_inc(trig_ready, 1)
            f(cosd[:, :, 1, :], red[:, 1], ACT.Sin).then_inc(trig_ready, 1)
            for c in range(CC):
                act.wait_ge(pair_ready, max(c + 1, 2))
                if c >= 2:
                    act.wait_ge(glu_done, c - 1)
                f(sgl[:, c % 2, :], ps[:, 2 * c + 1, :], ACT.Sigmoid).then_inc(sg_ready, 1)
            for j in range(4):
                act.wait_ge(lat_ready, j + 1)
                f(latsq[:, j, :], ps[:, j, :], ACT.Square).then_inc(lat_sq, 1)
                f(latT[:, j, :], ps[:, j, :], ACT.Copy, scale=vcol[:, V_QL + j:V_QL + j + 1]).then_inc(lat_done, 1)
            act.wait_ge(krope_ready, 1)
            f(krope[:].rearrange("p t r -> p (t r)"), ps[:, 4, 0:TT * ROPE], ACT.Copy).then_inc(krope_copied, 1)
            act.wait_ge(lat_ss, 1)
            f(lat_std[:, 0:4], ps[:, 5, 0:4], ACT.Sqrt, bias=eps[:, 0:1], scale=1.0 / Q_RANK)
            f(lat_std[:, 4:8], ps[:, 5, 4:8], ACT.Sqrt, bias=eps[:, 0:1], scale=1.0 / KV_RANK).then_inc(lat_std_ready, 1)

            def rows_to_sbuf(u):
                t, b, r = u // 2, unit_bank[u], rows[u]
                act.wait_ge(rows_ready, u + 1)
                if u % 2 == 0:
                    for half in range(2):
                        last = f(r[:, half * 4:half * 4 + 4, :], ps[:, b + half, 0:Q_RANK].rearrange("p (h d) -> p h d", d=HD),
                                 ACT.Copy, scale=lat_rs[:, t:t + 1])
                else:
                    for half in range(2):
                        src = ps[:, b + half, :].rearrange("p (h d) -> p h d", d=NOPE + VD)
                        f(r[:, half * 4:half * 4 + 4, 0:NOPE], src[:, :, 0:NOPE], ACT.Copy, scale=lat_rs[:, 4 + t:5 + t])
                        f(vrow[:, t, half * 256:(half + 1) * 256].rearrange("p (h d) -> p h d", d=VD), src[:, :, NOPE:],
                          ACT.Copy, scale=lat_rs[:, 4 + t:5 + t])
                    last = f(r[:, :, NOPE:], krope[:, t, :].unsqueeze(1).broadcast_to([P, H, ROPE]), ACT.Copy)
                last.then_inc(rows_out, 1)

            def squares(u):
                act.wait_ge(rows_out, u + 1)
                if u >= 2:
                    act.wait_ge(hss_ready, u - 1)
                f(rowsq[:, u % 2, :], rows[u][:].rearrange("p h d -> p (h d)"), ACT.Square).then_inc(rowsq_ready, 1)

            def head_std(lo):
                act.wait_ge(hss_ready, lo + 4)
                f(hstd[:, lo:lo + 4, :], hss[:, lo:lo + 4, :], ACT.Sqrt, bias=eps[:, 0:1], scale=1.0 / HD).then_inc(hstd_ready, 1)

            act.wait_ge(lat_rs_ready, 1)
            for u in range(2):
                rows_to_sbuf(u)
                squares(u)
            rows_to_sbuf(2)
            rows_to_sbuf(3)
            act.wait_ge(ln_xc, 1)
            f(lnsq[:], cacc[:], ACT.Square).then_inc(ln_sq, 1)
            squares(2)
            squares(3)
            act.wait_ge(ln_var, 1)
            f(ln_std[:], ps[:, 5, :], ACT.Sqrt, bias=eps[:, 0:1]).then_inc(ln_stdr, 1)
            head_std(0)
            rows_to_sbuf(4)
            squares(4)
            act.wait_ge(ln_norm, 1)
            for c in range(CC):
                last = f(cacc[:, c, :], cacc[:, c, :], ACT.Identity, bias=vcol[:, V_LNB + c:V_LNB + c + 1],
                         scale=vcol[:, V_LNG + c:V_LNG + c + 1])
            st.settle(last)
            f(lnsq[:], cacc[:], ACT.Sigmoid).then_inc(ln_sig, 1)
            rows_to_sbuf(5)
            squares(5)
            rows_to_sbuf(6)
            squares(6)
            rows_to_sbuf(7)
            squares(7)
            act.wait_ge(ln_silu, 1)
            f(lnsq[:], cacc[:], ACT.Square).then_inc(conv_sq, 1)
            head_std(4)
            for c in range(CC):
                f(mixT[:, 4 + c, :], cacc[:, c, :], ACT.Copy, scale=vcol[:, V_CG + c:V_CG + c + 1]).then_inc(conv_mix, 1)
            act.wait_ge(conv_ss, 1)
            f(css[:], ps[:, 5, 0:TT], ACT.Sqrt, bias=eps[:, 0:1], scale=1.0 / CONV).then_inc(conv_std, 1)
            for w in range(2 * TT):
                act.wait_ge(rows_turned, w + 1)
                dst = qT if w % 2 == 0 else kT
                for half in range(2):
                    last = f(dst[:, half * 4:half * 4 + 4, (w // 2) * P:(w // 2 + 1) * P],
                             ps[0:HD, turn_bank(w) + half, :].rearrange("p (h t) -> p h t", t=P), ACT.Copy)
                last.then_inc(rowsT_out, 1)
            for s in range(TT * H + 1):
                if s < TT * H:
                    act.wait_ge(max_ready, s + 1)
                    if s >= 2:
                        act.wait_ge(pT_ready, s - 1)
                    w = (s // H + 1) * P
                    f(probs[:, s % 2, 0:w], ps[:, s % 2, 0:w], ACT.Exp, bias=nmx[:, s:s + 1], scale=SCALE,
                      accum_out=den[:, s // H, s % H:s % H + 1]).then_inc(exp_ready, 1)
                if s >= 1:
                    z = s - 1
                    act.wait_ge(pT_ready, z + 1)
                    if z >= 2:
                        act.wait_ge(pv_done, z - 1)
                    w = z // H + 1
                    f(probsT[:, z % 2, 0:w, :], ps[:, 2 + z % 2, 0:w * P].rearrange("p (n q) -> p n q", q=P),
                      ACT.Copy).then_inc(pT_out, 1)
            act.wait_ge(a_ss_ready, TT)
            f(astd[:], ass_[:], ACT.Sqrt, bias=eps[:, 0:1], scale=1.0 / (H * VD)).then_inc(a_std_ready, 1)
            for t in range(TT):
                act.wait_ge(x1_ready, t + 1)
                st.settle(f(hn[:, t, :], x[:, t, :], ACT.Square, accum_out=ss1[:, t:t + 1]))
                f(std1[:, t:t + 1], ss1[:, t:t + 1], ACT.Sqrt, bias=eps[:, 0:1], scale=1.0 / D).then_inc(std1_ready, 1)
                act.wait_ge(hn_turned, t + 1)
                if t >= 2:
                    act.wait_ge(log_ready, t - 1)
                f(h2T[:, t % 2, 0:4, :], ps[:, 4 * (t % 2), :].rearrange("p (k q) -> p k q", q=P), ACT.Copy).then_inc(h2_act, 1)
            act.wait_ge(topd_ready, 1)
            f(tg[:], tg[:], ACT.Exp).then_inc(texp_ready, 1)
            act.wait_ge(bias_landed, 64)
            act.wait_ge(out_ready, TT)
            f(bias_hl[:], bias_raw[:], ACT.Copy).then_inc(bias_hi_ready, 1)
            act.wait_ge(bias_ready, 1)
            act.wait_ge(hn_ready, TT)
            for q in range(SPLIT):
                act.wait_ge(landed[q], 32)
                if q == SPLIT - 1:
                    act.wait_ge(stored, 16 * 2 * (TT + 1))
                f(w_hi[q][:], raw[q][:], ACT.Copy).then_inc(hi_done, 1)

            def high_part(i, q):
                act.wait_ge(landed[q % RAW], i * 64 + (q // RAW * 32 + 32))
                act.wait_ge(split_free, i * CHUNKS + (q + 1))
                f(w_hi[q % SPLIT][:], raw[q % RAW][:], ACT.Copy).then_inc(hi_done, 1)

            def high_x(i):
                act.wait_ge(x_turned, i + 1)
                f(x_hi[:].rearrange("p k q -> p (k q)"), ps[:, 6:8, :].rearrange("p a b -> p (a b)"), ACT.Copy).then_inc(x_hi_ready, 1)

            def high_act(half, count):
                act.wait_ge(act_turned, count)
                f(a_hi[:, 4 * half:4 * half + 4, :].rearrange("p k q -> p (k q)"), ps[:, 7 - half, :], ACT.Copy).then_inc(a_hi_ready, 1)

            def sigmoid(count):
                act.wait_ge(gmin_ready, count)
                f(g_sig[:], g_in[:], ACT.Sigmoid, scale=ALPHA).then_inc(sig_ready, 1)

            def rows_of_y(count, i, q):
                act.wait_ge(hold_ready, count)
                act.wait_ge(split_free, multiplied(i, q))
                f(yrow[:], ps[:, 4:6, :].rearrange("p a b -> p (a b)"), ACT.Identity, scale=gate_hold[:, 0:1]).then_inc(yrow_ready, 1)

            act.wait_ge(tab_ready, 1)
            n_tiles = act.value_load(tab[0:1, TAB_T + E:TAB_T + E + 1], min_val=E, max_val=MAX_TILES)
            with act.Fori(0, MAX_TILES) as i:
                with act.If(i < n_tiles):
                    with act.If(i > 0):
                        high_part(i, 0)
                    high_x(i)
                    sigmoid(i * 2 + 1)
                    with act.If(i > 0):
                        for q in (1, 2, 3):
                            high_part(i, q)
                    high_part(i, 4)
                    high_act(1, i * 2 + 1)
                    for q in (5, 6):
                        high_part(i, q)
                    sigmoid(i * 2 + 2)
                    for q in (7, 8):
                        high_part(i, q)
                    rows_of_y(i + 1, i, DN1[-1])
                    for q in (9, 10):
                        high_part(i, q)
                    high_act(0, i * 2 + 2)
                    high_part(i, 11)
            sigmoid(n_tiles * 2 + 1)
            high_part(n_tiles, 0)
            high_part(n_tiles, 1)
            high_act(1, n_tiles * 2 + 1)
            rows_of_y(n_tiles + 1, n_tiles, 1)

        @block.vector
        def _(dve):
            v = nc.vector
            st = Steps(dve, dve_step)

            dve.wait_ge(small_landed, 16 * N_SMALL)
            v.tensor_copy(pos_f[:], pos_i[:]).then_inc(posf_ready, 1)
            dve.wait_ge(cols_turned, 1)
            v.tensor_copy(vcol[:], ps[:, 7, 0:V_ALL]).then_inc(cols_ready, 1)
            dve.wait_ge(cols_ready, 1)
            for t in range(TT):
                dve.wait_ge(xstd_ready, t + 1)
                st.settle(v.reciprocal(rsx[:, t:t + 1], stdx[:, t:t + 1]))
                v.tensor_scalar(xn[:, t, :], x[:, t, :], rsx[:, t:t + 1], None, ALU.mult).then_inc(xn_ready, 1)
            dve.wait_ge(x_turned0, 1)
            for k in range(0, DK, 2):
                v.tensor_scalar(hT[:, k, :], ps[:, k, :], vcol[:, V_MIX + k:V_MIX + k + 1], None, ALU.mult).then_inc(hT_dve, 1)

            dve.wait_ge(consts, 13 + ROPE // 2)
            st.settle(v.tensor_tensor(ang[:], vcol[:, V_POS:V_ALL].unsqueeze(2).broadcast_to([P, TT, 16]),
                                      inv_freq[:].unsqueeze(1).broadcast_to([P, TT, 16]), ALU.mult))
            for c in range(2):
                n_, r_ = turns[:, c], red[:, c]
                st.settle(v.tensor_scalar(n_, ang[:], 1.0 / TWO_PI, 0.25 * c, ALU.mult, ALU.add))
                st.settle(v.tensor_scalar(n_, n_, ROUND, ROUND, ALU.add, ALU.subtract))
                st.settle(v.scalar_tensor_tensor(out=r_, in0=n_, scalar=-PI2_A, in1=ang[:], op0=ALU.mult, op1=ALU.add))
                st.settle(v.scalar_tensor_tensor(out=r_, in0=n_, scalar=-PI2_B, in1=r_, op0=ALU.mult, op1=ALU.add))
                st.settle(v.scalar_tensor_tensor(out=r_, in0=n_, scalar=-PI2_C, in1=r_, op0=ALU.mult, op1=ALU.add))
                st.settle(v.tensor_scalar(r_, r_, 0.5 * np.pi * c, PI_IN, ALU.add, ALU.min))
                last = v.tensor_scalar(r_, r_, -PI_IN, None, ALU.max)
                if c == 0:
                    st.settle(last)
            last.then_inc(ang_ready, 1)
            dve.wait_ge(trig_ready, 3)
            st.settle(v.tensor_scalar(nsin[:], sin_[:], -1.0, None, ALU.mult))
            v.tensor_copy(pick[0:E], ident[0:E, 0:E])
            v.tensor_copy(pick[E:2 * E], ident[E:2 * E, E:2 * E])

            for pair in range(2):
                for c in (2 * pair, 2 * pair + 1):
                    dve.wait_ge(sg_ready, c + 1)
                    v.tensor_tensor(ypad[:, c, PAD:], ps[:, 2 * c, :], sgl[:, c % 2, :], ALU.mult).then_inc(glu_done, 1)
                dve.wait_ge(glu_done, 2 * pair + 2)
                before = {}
                for j in range(TAPS):
                    if pair == 1 and j == TAPS - 6:
                        dve.wait_ge(lat_std_ready, 1)
                        v.reciprocal(lat_rs[:], lat_std[:]).then_inc(lat_rs_ready, 1)
                    for c in (2 * pair, 2 * pair + 1):
                        w = vcol[:, V_W + j * CC + c:V_W + j * CC + c + 1]
                        if j == 0:
                            ins = v.tensor_scalar(cacc[:, c, :], ypad[:, c, 0:T], w, vcol[:, V_DWB + c:V_DWB + c + 1],
                                                  ALU.mult, ALU.add)
                        else:
                            dve.wait_ge(dve_step, before[c])
                            ins = v.scalar_tensor_tensor(out=cacc[:, c, :], in0=ypad[:, c, j:j + T], scalar=w,
                                                         in1=cacc[:, c, :], op0=ALU.mult, op1=ALU.add)
                        before[c] = st.mark(ins)
                dve.wait_ge(dve_step, st.n)
            dve.sem_inc(conv_done, 1)

            def head_sums(*units):
                for u in units:
                    dve.wait_ge(rowsq_ready, u + 1)
                    v.tensor_reduce(hss[:, u, :], rowsq[:, u % 2, :].rearrange("p (h d) -> p h d", d=HD), AX.X,
                                    ALU.add).then_inc(hss_ready, 1)

            def head_rs(lo):
                dve.wait_ge(hstd_ready, lo // 4 + 1)
                st.settle(v.reciprocal(hrs[:, lo:lo + 4, :], hstd[:, lo:lo + 4, :]))

            def head_norm(u):
                v.tensor_tensor(rows[u][:], rows[u][:], hrs[:, u, :].unsqueeze(2).broadcast_to([P, H, HD]),
                                ALU.mult).then_inc(headnorm, 1)

            def rotate(u):
                t, r = u // 2, rows[u]
                dve.wait_ge(gained, u + 1)
                if u:
                    dve.wait_ge(roped, u)
                v.tensor_tensor(rtmp[:, 0], r[:, :, NOPE:], cosd[:, t].rearrange("p a b -> p (a b)").unsqueeze(1).broadcast_to([P, H, ROPE]), ALU.mult)
                v.tensor_tensor(rtmp[:, 1, :, 0:16], r[:, :, NOPE + 16:], nsin[:, t, :].unsqueeze(1).broadcast_to([P, H, 16]), ALU.mult)
                st.settle(v.tensor_tensor(rtmp[:, 1, :, 16:32], r[:, :, NOPE:NOPE + 16], sin_[:, t, :].unsqueeze(1).broadcast_to([P, H, 16]), ALU.mult))
                v.tensor_tensor(r[:, :, NOPE:], rtmp[:, 0], rtmp[:, 1], ALU.add).then_inc(roped, 1)

            dve.wait_ge(ln_mean, 1)
            v.tensor_tensor(cacc[:], cacc[:], ps[:, 4, :].unsqueeze(1).broadcast_to([P, CC, T]), ALU.subtract).then_inc(ln_xc, 1)
            head_sums(0, 1, 2, 3)
            dve.wait_ge(ln_stdr, 1)
            st.settle(v.reciprocal(ln_std[:], ln_std[:]))
            v.tensor_tensor(cacc[:], cacc[:], ln_std[:].unsqueeze(1).broadcast_to([P, CC, T]), ALU.mult).then_inc(ln_norm, 1)
            head_rs(0)
            head_norm(0)
            head_norm(1)
            head_sums(4)
            rotate(0)
            head_norm(2)
            rotate(1)
            head_norm(3)
            dve.wait_ge(ln_sig, 1)
            v.tensor_tensor(cacc[:], cacc[:], lnsq[:], ALU.mult).then_inc(ln_silu, 1)
            head_sums(5)
            rotate(2)
            head_sums(6)
            rotate(3)
            head_sums(7)
            head_rs(4)
            head_norm(4)
            for u in range(4, 8):
                if u < 7:
                    head_norm(u + 1)
                rotate(u)
            dve.wait_ge(conv_std, 1)
            st.settle(v.reciprocal(c_rs[:], css[:]))

            def add_conv(t):
                dve.wait_ge(conv_out, t + 1)
                for half in range(2):
                    xs = x[:, t, half * 512:(half + 1) * 512]
                    last = v.scalar_tensor_tensor(out=xs, in0=ps[:, (2 if t == 0 else 6) + half, :], scalar=c_rs[:, t:t + 1],
                                                  in1=xs, op0=ALU.mult, op1=ALU.add)
                last.then_inc(conv_added, 1)

            add_conv(0)
            add_conv(1)

            def row_max(s):
                w = (s // H + 1) * P
                dve.wait_ge(s_ready, s + 1)
                st.settle(v.memset(ps[0:CHUNK, s % 2, w - CHUNK:w], -1e30))
                st.settle(v.tensor_reduce(mx[:, s:s + 1], ps[:, s % 2, 0:w], AX.X, ALU.max))
                v.tensor_scalar(nmx[:, s:s + 1], mx[:, s:s + 1], -SCALE, None, ALU.mult).then_inc(max_ready, 1)

            def normalise(qb):
                dve.wait_ge(pv_done, (qb + 1) * H)
                st.settle(v.reciprocal(rden[:, qb, :], den[:, qb, :]))
                if qb >= 2:
                    dve.wait_ge(o_turned, qb - 1)
                v.tensor_tensor(attn_row[:, qb % 2, :].rearrange("p (h d) -> p h d", d=VD),
                                ps[:, 4 + qb % 2, :].rearrange("p (h d) -> p h d", d=VD),
                                rden[:, qb, :].unsqueeze(2).broadcast_to([P, H, VD]), ALU.mult).then_inc(o_normed, 1)
                dve.wait_ge(o_normed, qb + 1)
                v.tensor_tensor_reduce(out=ln_std[:], in0=attn_row[:, qb % 2, :], in1=attn_row[:, qb % 2, :], scale=1.0,
                                       scalar=0.0, op0=ALU.mult, op1=ALU.add, accum_out=ass_[:, qb:qb + 1]).then_inc(a_ss_ready, 1)

            def mix(qb):
                dve.wait_ge(o_turned, qb + 1)
                v.tensor_tensor(mixT[:, 0:4, qb * P:(qb + 1) * P], ps[:, 4 + qb % 2, :].rearrange("p (n q) -> p n q", q=P),
                                vcol[:, V_AG:V_AG + 4].unsqueeze(2).broadcast_to([P, 4, P]), ALU.mult).then_inc(attn_mix, 1)

            for s in range(TT * H + 7):
                if s < TT * H:
                    row_max(s)
                if s in (8, 17):
                    add_conv(s // 9 + 2)
                if s >= 11 and (s - 11) % H == 0:
                    normalise((s - 11) // H)
                if s >= 14 and (s - 14) % H == 0:
                    mix((s - 14) // H)

            dve.wait_ge(a_std_ready, 1)
            st.settle(v.reciprocal(a_rs[:], astd[:]))

            def residual(t):
                b = 4 * (t % 2)
                dve.wait_ge(out_ready, t + 1)
                for half in range(2):
                    xs = x[:, t, half * 512:(half + 1) * 512]
                    last = v.scalar_tensor_tensor(out=xs, in0=ps[:, b + half, :], scalar=a_rs[:, t:t + 1],
                                                  in1=xs, op0=ALU.mult, op1=ALU.add)
                last.then_inc(x1_ready, 1)

            def norm_ffn(t):
                dve.wait_ge(std1_ready, t + 1)
                dve.wait_ge(gain_landed, 16)
                st.settle(v.reciprocal(rs1[:, t:t + 1], std1[:, t:t + 1]))
                v.scalar_tensor_tensor(out=hn[:, t, :], in0=x[:, t, :], scalar=rs1[:, t:t + 1], in1=ffn_gain[:],
                                       op0=ALU.mult, op1=ALU.mult).then_inc(hn_ready, 1)

            def turned_out(t):
                dve.wait_ge(hn_turned, t + 1)
                if t >= 2:
                    dve.wait_ge(log_ready, t - 1)
                v.tensor_copy(h2T[:, t % 2, 4:8, :], ps[:, 4 * (t % 2) + 1, :].rearrange("p (k q) -> p k q", q=P)).then_inc(h2_dve, 1)

            def logits_out(t):
                dve.wait_ge(log_ready, t + 1)
                v.tensor_tensor(logits[:, t, :], ps[:, 4 * (t % 2) + 2, 0:E], router_bias[:], ALU.add).then_inc(log_out, 1)

            for t in range(TT):
                residual(t)
                norm_ffn(t)
                turned_out(t)
                logits_out(t)

            dve.wait_ge(log_out, TT)
            for t in range(TT):
                st.settle(v.max(top_v[:, t, :], logits[:, t, :]))
                st.settle(v.max_index(top_i[:, t, :], top_v[:, t, :], logits[:, t, :]))
            v.tensor_tensor(tg[:], top_v[:, :, 0:TOPK], top_v[:, :, 0:1].broadcast_to([P, TT, TOPK]), ALU.subtract).then_inc(topd_ready, 1)
            st.settle(v.tensor_copy(top_f[:], top_i[:, :, 0:TOPK]))
            st.settle(v.tensor_tensor(hot[:], iota_s[:, 0:E].unsqueeze(1).broadcast_to([P, 16, E]),
                                      top_f[:].rearrange("p t k -> p (t k)").unsqueeze(2).broadcast_to([P, 16, E]), ALU.is_equal))
            v.tensor_reduce(mask[:], hot[:].rearrange("p (t k) e -> p t e k", k=TOPK), AX.X, ALU.add).then_inc(mask_ready, 1)
            dve.wait_ge(texp_ready, 1)
            st.settle(v.tensor_reduce(tgs[:], tg[:], AX.X, ALU.add))
            st.settle(v.reciprocal(tgr[:], tgs[:]))
            st.settle(v.tensor_tensor(tg[:], tg[:], tgr[:].unsqueeze(2).broadcast_to([P, TT, TOPK]), ALU.mult))
            st.settle(v.tensor_tensor(hotg[:], hot[:], tg[:].rearrange("p t k -> p (t k)").unsqueeze(2).broadcast_to([P, 16, E]), ALU.mult))
            st.settle(v.tensor_reduce(gate[:], hotg[:].rearrange("p (t k) e -> p t e k", k=TOPK), AX.X, ALU.add))
            dve.wait_ge(pos_ready, 1)
            st.settle(v.tensor_copy(cnt[:, 0:1], ps[0:E, 1, 0:1]))
            st.settle(v.tensor_scalar(cnt[:, 1:2], cnt[:, 0:1], float(P), 1.0, ALU.is_gt, ALU.add))
            st.settle(v.scalar_tensor_tensor(out=cnt[:, 1:2], in0=cnt[:, 0:1], scalar=2.0 * P, in1=cnt[:, 1:2], op0=ALU.is_gt, op1=ALU.add))
            v.scalar_tensor_tensor(out=cnt[:, 1:2], in0=cnt[:, 0:1], scalar=3.0 * P, in1=cnt[:, 1:2], op0=ALU.is_gt, op1=ALU.add).then_inc(nt_ready, 1)
            st.settle(v.scalar_tensor_tensor(out=posm[:].rearrange("p t e -> p (t e)"), in0=ps[:, 0, 0:TT * E], scalar=NONE,
                                             in1=mask[:].rearrange("p t e -> p (t e)"), op0=ALU.add, op1=ALU.mult))
            st.settle(v.tensor_scalar(posm[:], posm[:], NONE, None, ALU.subtract))
            dve.wait_ge(start_ready, 1)
            st.settle(v.tensor_copy(cnt[:, 2:3], ps[0:E, 1, 4:5]))
            st.settle(v.tensor_tensor(cnt[:, 3:4], cnt[:, 2:3], cnt[:, 1:2], ALU.add))
            it = iota_s[0:E, 0:TAB]
            st.settle(v.tensor_scalar(memj[:], it, cnt[:, 2:3], None, ALU.is_ge))
            st.settle(v.scalar_tensor_tensor(out=member[:], in0=it, scalar=cnt[:, 3:4], in1=memj[:], op0=ALU.is_lt, op1=ALU.mult))
            st.settle(v.scalar_tensor_tensor(out=memj[:], in0=it, scalar=cnt[:, 2:3], in1=member[:], op0=ALU.subtract, op1=ALU.mult))
            st.settle(v.tensor_scalar(memn[:], memj[:], -float(P), cnt[:, 0:1], ALU.mult, ALU.add))
            v.tensor_tensor(memn[:], memn[:], member[:], ALU.mult).then_inc(mem_ready, 1)
            dve.wait_ge(fields_ready, 1)
            v.tensor_copy(tab[0:1, 0:TAB_T], ps[0:1, 2, 0:TAB_T])
            st.settle(v.tensor_copy(tab[0:1, TAB_T:TAB_T + E + 1], ps[0:1, 1, 8:8 + E + 1]))
            v.memset(ps[:, 2:4, :], 0.0)
            st.settle(v.memset(ps[:, 4:6, :], 0.0))
            dve.sem_inc(tab_ready, 1)

            def slots_of(tile, steps):
                e = dve.value_load(tab[0:1, bass.ds(tile + TAB_E, 1)], min_val=0, max_val=E - 1)
                j = dve.value_load(tab[0:1, bass.ds(tile + TAB_J, 1)], min_val=0, max_val=3)
                v.tensor_tensor(onehot[:], iota_s[:, bass.ds(j * P, P)].unsqueeze(1).broadcast_to([P, TT, P]),
                                posm[:, :, bass.ds(e, 1)].broadcast_to([P, TT, P]), ALU.is_equal)
                v.tensor_copy(tokv[:, :, 2:3], gate[:, :, bass.ds(e, 1)]).then_inc(hot_ready, 1)

            def slots_to_sbuf(steps):
                v.tensor_copy(gate_next[:], ps[:, 6, 2:3])
                steps(v.tensor_scalar(slot_f[:, 0:1], ps[:, 6, 1:2], -1.0, 1.0, ALU.mult, ALU.add))
                steps(v.scalar_tensor_tensor(out=slot_f[:, 1:2], in0=slot_f[:, 0:1], scalar=slot_row[:, 0:1],
                                             in1=ps[:, 6, 0:1], op0=ALU.mult, op1=ALU.add))
                v.tensor_copy(idx_next[:], slot_f[:, 1:2]).then_inc(slots_out, 1)

            def low_part(i, q):
                dve.wait_ge(hi_done, i * CHUNKS + (q + 1))
                v.tensor_tensor(w_lo[q % SPLIT][:], raw[q % RAW][:], w_hi[q % SPLIT][:].bitcast(F32),
                                ALU.subtract).then_inc(raw_free[q % RAW], 1)

            def low_x(i):
                dve.wait_ge(x_hi_ready, i + 1)
                v.tensor_tensor(x_lo[:].rearrange("p k q -> p (k q)"), ps[:, 6:8, :].rearrange("p a b -> p (a b)"),
                                x_hi[:].rearrange("p k q -> p (k q)").bitcast(F32), ALU.subtract).then_inc(x_ready, 1)

            def low_act(half, count):
                dve.wait_ge(a_hi_ready, count)
                ks = slice(4 * half, 4 * half + 4)
                v.tensor_tensor(a_lo[:, ks, :].rearrange("p k q -> p (k q)"), ps[:, 7 - half, :],
                                a_hi[:, ks, :].rearrange("p k q -> p (k q)").bitcast(F32), ALU.subtract).then_inc(a_ready, 1)

            def swiglu(half, count, done, steps):
                dve.wait_ge(split_free, done)
                v.tensor_scalar(g_in[:], ps[:, 2 * half, :], LIMIT, None, ALU.min).then_inc(gmin_ready, 1)
                v.tensor_scalar(u_in[:], ps[:, 2 * half + 1, :], LIMIT, -LIMIT, ALU.min, ALU.max)
                dve.wait_ge(sig_ready, count)
                steps(v.tensor_tensor(g_in[:], g_in[:], g_sig[:], ALU.mult))
                v.scalar_tensor_tensor(out=act_row[:], in0=u_in[:], scalar=1.0, in1=g_in[:],
                                       op0=ALU.add, op1=ALU.mult).then_inc(act_ready, 1)

            n_tiles = dve.value_load(tab[0:1, TAB_T + E:TAB_T + E + 1], min_val=E, max_val=MAX_TILES)
            slots_of(0, st.settle)
            dve.wait_ge(slots_ready, 1)
            slots_to_sbuf(st.settle)
            dve.sem_inc(hold_ready, 1)

            LOOP_STEPS = 6

            with dve.Fori(0, MAX_TILES) as i:
                with dve.If(i < n_tiles):
                    count = [0]

                    def steps(ins):
                        count[0] += 1
                        ins.then_inc(moe_step, 1)
                        dve.wait_ge(moe_step, i * LOOP_STEPS + count[0])

                    e = dve.value_load(tab[0:1, bass.ds(i + TAB_E, 1)], min_val=0, max_val=E - 1)
                    dve.wait_ge(sel_used, i + 1)
                    v.tensor_copy(sel[:], pick[:, bass.ds(e, 1)].broadcast_to([2 * E, P])).then_inc(sel_ready, 1)
                    low_x(i)
                    swiglu(1, i * 2 + 1, i * CHUNKS + (GU1[-1] + 1 + SPLIT - CHUNKS), steps)
                    with dve.If(i > 0):
                        for q in (1, 2):
                            low_part(i, q)
                    slots_of(i + 1, steps)
                    with dve.If(i > 0):
                        low_part(i, 3)
                    low_act(1, i * 2 + 1)
                    for q in (5, 6):
                        low_part(i, q)
                    swiglu(0, i * 2 + 2, multiplied(i, GU0[-1]), steps)
                    low_part(i, 7)
                    v.tensor_copy(gate_cur[:], gate_next[:])
                    steps(v.tensor_copy(idx_cur[:], idx_next[:]))
                    dve.wait_ge(slots_ready, i + 2)
                    dve.wait_ge(gathered, i * 16 + 16)
                    slots_to_sbuf(steps)
                    for q in (8, 9, 10):
                        low_part(i, q)
                    low_act(0, i * 2 + 2)
                    low_part(i, 11)
                    dve.wait_ge(scattered, i * 16 + 16)
                    v.tensor_copy(gate_hold[:], gate_cur[:])
                    steps(v.tensor_copy(idx_hold[:], idx_cur[:]))
                    dve.sem_inc(hold_ready, 1)
            assert count[0] == LOOP_STEPS
            swiglu(1, n_tiles * 2 + 1, n_tiles * CHUNKS + (GU1[-1] + 1 + SPLIT - CHUNKS), st.settle)
            low_part(n_tiles, 0)
            low_part(n_tiles, 1)
            low_act(1, n_tiles * 2 + 1)


_INS = ["x", "positions", "norm_mix_g", "w_in", "q_latent_g", "w_uq", "kv_latent_g", "w_ukv", "q_head_g", "k_head_g",
        "conv_dw_w", "conv_dw_b", "conv_ln_g", "conv_ln_b", "attn_out_g", "conv_out_g", "w_out", "norm_ffn_g",
        "router_w", "router_b", "w_gate_up", "b_gate_up", "w_down", "b_down"]


def kernel(**inputs):
    import numpy as _np
    import concourse.bacc as _bacc
    from concourse import mybir as _mybir
    from concourse.bass_utils import run_bass_kernel_spmd as _run

    nc = _bacc.Bacc("TRN2", target_bir_lowering=False, num_devices=1)
    arrays, args = {}, {}
    for name in _INS:
        a = _np.ascontiguousarray(inputs[name])
        arrays[f"in_{name}"] = a
        args[name] = nc.dram_tensor(f"in_{name}", a.shape, _mybir.dt.from_np(a.dtype), kind="ExternalInput").ap()
    args["out"] = nc.dram_tensor("out_0", (1, T, D), _mybir.dt.float32, kind="ExternalOutput").ap()
    block_kernel(nc, args)
    r = _run(nc, [arrays], core_ids=[0])
    return r.results[0]["out_0"]
```
